# Optimizing a Trainium2 kernel written in Bass

```python
import math
import jax, jax.numpy as jnp
from jax import lax
import numpy as np

D_MODEL = 2048
BATCH = 1
SEQ = 256
DEPTH = 2

MEM_LEN = 256
N_EVEN = (DEPTH + 1) // 2
N_ODD = DEPTH // 2
WIDTH_A = D_MODEL // 2
WIDTH_B = D_MODEL // 2
POOL_WINDOWS = (2, 4, 8, 16)
N_POOL_GROUPS = len(POOL_WINDOWS)
POOL_GROUP = WIDTH_A // N_POOL_GROUPS
HGRN_HEAD_DIM = 128
HGRN_HEADS = WIDTH_B // HGRN_HEAD_DIM
HGRN_CHUNK = 32
SB_HEAD_DIM = 128
SB_HEADS = D_MODEL // SB_HEAD_DIM
SB_BLOCK = 128
XA_HEADS = 4
XA_HEAD_DIM = D_MODEL // XA_HEADS
EVEN_IN = 2 * WIDTH_A + 4 * WIDTH_B
ODD_IN = 4 * D_MODEL
EPS = 1e-6

kernel_name = 'hybrid_pool_hgrn2_stickbreak_block'

def rms_norm(x, g):
    xf = x.astype(jnp.float32)
    y = xf * lax.rsqrt(jnp.mean(xf * xf, axis=-1, keepdims=True) + EPS)
    return (y * g.astype(jnp.float32)).astype(x.dtype)

def pool_mixer(u, w, scale):
    B, S, _ = u.shape
    ug = u.astype(jnp.float32).reshape(B, S, N_POOL_GROUPS, POOL_GROUP)
    cs = jnp.cumsum(ug, axis=1)
    pooled = []
    for gi, win in enumerate(POOL_WINDOWS):
        c = cs[:, :, gi]
        shifted = jnp.pad(c, ((0, 0), (win, 0), (0, 0)))[:, :S]
        cnt = jnp.minimum(jnp.arange(1, S + 1), win).astype(jnp.float32)
        pooled.append((c - shifted) / cnt[None, :, None])
    mixed = jnp.stack(pooled, axis=2) - ug
    y = jnp.einsum('bsgc,gcd->bsgd', mixed, w.astype(jnp.float32))
    y = y.reshape(B, S, WIDTH_A) * scale.astype(jnp.float32)
    return y.astype(u.dtype)

def hgrn2(q, f_logit, inp, lb, norm_g):
    B, S, _ = q.shape
    H, D, C = HGRN_HEADS, HGRN_HEAD_DIM, HGRN_CHUNK
    N = S // C
    f32 = jnp.float32
    f = lb + (1.0 - lb) * jax.nn.sigmoid(f_logit.astype(f32))
    logf = jnp.log(f)
    k = 1.0 - f

    def heads(t):
        return t.astype(f32).reshape(B, N, C, H, D).transpose(0, 3, 1, 2, 4)

    qh, kh, ih, lfh = heads(q), heads(k), heads(inp), heads(logf)
    bcum = jnp.cumsum(lfh, axis=3)
    q_t = qh * jnp.exp(bcum)
    k_t = kh * jnp.exp(-bcum)
    causal = jnp.tril(jnp.ones((C, C), dtype=bool))
    scores = jnp.where(causal, jnp.einsum('bhncd,bhnsd->bhncs', q_t, k_t), 0.0)
    o_intra = jnp.einsum('bhncs,bhnsv->bhncv', scores, ih)
    b_last = bcum[:, :, :, -1]
    k_end = kh * jnp.exp(b_last[:, :, :, None, :] - bcum)
    U = jnp.einsum('bhnsd,bhnsv->bhndv', k_end, ih)
    decay = jnp.exp(b_last)

    def step(state, xs):
        d, u = xs
        return d[..., None] * state + u, state

    s0 = jnp.zeros((B, H, D, D), f32)
    _, s_prev = lax.scan(step, s0, (decay.transpose(2, 0, 1, 3), U.transpose(2, 0, 1, 3, 4)))
    s_prev = s_prev.transpose(1, 2, 0, 3, 4)
    o = o_intra + jnp.einsum('bhncd,bhndv->bhncv', q_t, s_prev)
    o = o.transpose(0, 2, 3, 1, 4).reshape(B, S, H, D)
    o = o * lax.rsqrt(jnp.mean(o * o, axis=-1, keepdims=True) + EPS)
    o = o * norm_g.astype(f32).reshape(H, D)
    return o.reshape(B, S, WIDTH_B).astype(q.dtype)

def stick_breaking_attention(q, k, v):
    S = q.shape[2]
    scale = 1.0 / math.sqrt(SB_HEAD_DIM)
    outs = []
    for blk in range(S // SB_BLOCK):
        t0, t1 = blk * SB_BLOCK, (blk + 1) * SB_BLOCK
        qb, kb, vb = q[:, :, t0:t1], k[:, :, :t1], v[:, :, :t1]
        z = jnp.einsum('bhtd,bhsd->bhts', qb, kb).astype(jnp.float32) * scale
        mask = jnp.arange(t1)[None, :] < jnp.arange(t0, t1)[:, None]
        log_beta = jax.nn.log_sigmoid(z)
        log_keep = jnp.where(mask, jax.nn.log_sigmoid(-z), 0.0)
        rev = jnp.cumsum(log_keep[..., ::-1], axis=-1)[..., ::-1] - log_keep
        A = jnp.where(mask, jnp.exp(log_beta + rev), 0.0)
        outs.append(jnp.einsum('bhts,bhsd->bhtd', A.astype(vb.dtype), vb))
    return jnp.concatenate(outs, axis=2)

def cross_attention(h, m, wq, wkv, wo):
    B, S, _ = h.shape
    M = m.shape[1]
    q = (h @ wq).reshape(B, S, XA_HEADS, XA_HEAD_DIM)
    k, v = jnp.split(m @ wkv, 2, axis=-1)
    k = k.reshape(B, M, XA_HEADS, XA_HEAD_DIM)
    v = v.reshape(B, M, XA_HEADS, XA_HEAD_DIM)
    s = jnp.einsum('bshd,bmhd->bhsm', q, k).astype(jnp.float32) / math.sqrt(XA_HEAD_DIM)
    p = jax.nn.softmax(s, axis=-1).astype(v.dtype)
    o = jnp.einsum('bhsm,bmhd->bshd', p, v).reshape(B, S, D_MODEL)
    return o @ wo

def setup_inputs(seed: int = 0) -> dict:
    key = jax.random.key(seed)
    ks = jax.random.split(key, 20)
    f32 = jnp.float32
    nrm = lambda k, shape, s: jax.random.normal(k, shape, f32) * s
    return {
        'x': nrm(ks[0], (BATCH, SEQ, D_MODEL), 1.0),
        'mem': nrm(ks[1], (BATCH, MEM_LEN, D_MODEL), 1.0),
        'norm_mix_g': 1.0 + nrm(ks[2], (DEPTH, D_MODEL), 0.02),
        'norm_xa_g': 1.0 + nrm(ks[3], (DEPTH, D_MODEL), 0.02),
        'norm_mem_g': 1.0 + nrm(ks[4], (DEPTH, D_MODEL), 0.02),
        'final_norm_g': 1.0 + nrm(ks[5], (D_MODEL,), 0.02),
        'w_in_even': nrm(ks[6], (N_EVEN, D_MODEL, EVEN_IN), D_MODEL ** -0.5),
        'pool_w': nrm(ks[7], (N_EVEN, N_POOL_GROUPS, POOL_GROUP, POOL_GROUP), POOL_GROUP ** -0.5),
        'pool_scale': 1.0 + nrm(ks[8], (N_EVEN, WIDTH_A), 0.02),
        'hgrn_lower_bounds': nrm(ks[9], (N_EVEN + 1, WIDTH_B), 0.1),
        'hgrn_norm_g': 1.0 + nrm(ks[10], (N_EVEN, WIDTH_B), 0.02),
        'w_out_even': nrm(ks[11], (N_EVEN, WIDTH_A + WIDTH_B, D_MODEL), (WIDTH_A + WIDTH_B) ** -0.5),
        'w_in_odd': nrm(ks[12], (N_ODD, D_MODEL, ODD_IN), D_MODEL ** -0.5),
        'w_out_odd': nrm(ks[13], (N_ODD, D_MODEL, D_MODEL), D_MODEL ** -0.5),
        'xa_wq': nrm(ks[14], (DEPTH, D_MODEL, D_MODEL), D_MODEL ** -0.5),
        'xa_wkv': nrm(ks[15], (DEPTH, D_MODEL, 2 * D_MODEL), D_MODEL ** -0.5),
        'xa_wo': nrm(ks[16], (DEPTH, D_MODEL, D_MODEL), D_MODEL ** -0.5),
    }

def reference(x, mem, norm_mix_g, norm_xa_g, norm_mem_g, final_norm_g,
              w_in_even, pool_w, pool_scale, hgrn_lower_bounds, hgrn_norm_g, w_out_even,
              w_in_odd, w_out_odd, xa_wq, xa_wkv, xa_wo):
    B, S, _ = x.shape
    lb_table = jnp.cumsum(jax.nn.softmax(hgrn_lower_bounds.astype(jnp.float32), axis=0), axis=0)
    for l in range(DEPTH):
        h = rms_norm(x, norm_mix_g[l])
        if l % 2 == 0:
            e = l // 2
            u = h @ w_in_even[e]
            a_in, a_gate, b_q, b_f, b_i, b_gate = jnp.split(u, 6, axis=-1)
            y_a = pool_mixer(a_in, pool_w[e], pool_scale[e]) * jax.nn.silu(a_gate)
            y_b = hgrn2(b_q, b_f, b_i, lb_table[e], hgrn_norm_g[e]) * jax.nn.silu(b_gate)
            x = x + jnp.concatenate([y_a, y_b], axis=-1) @ w_out_even[e]
        else:
            o = l // 2
            u = h @ w_in_odd[o]
            q, k, v, gate = jnp.split(u, 4, axis=-1)
            sh = lambda t: t.reshape(B, S, SB_HEADS, SB_HEAD_DIM).transpose(0, 2, 1, 3)
            att = stick_breaking_attention(sh(q), sh(k), sh(v))
            att = att.transpose(0, 2, 1, 3).reshape(B, S, D_MODEL)
            x = x + (att * jax.nn.silu(gate)) @ w_out_odd[o]
        hx = rms_norm(x, norm_xa_g[l])
        hm = rms_norm(mem, norm_mem_g[l])
        x = x + cross_attention(hx, hm, xa_wq[l], xa_wkv[l], xa_wo[l])
    return rms_norm(x, final_norm_g)


_drawn_inputs = setup_inputs


def setup_inputs(seed=0):
    import zlib

    import numpy as np

    out = dict(_drawn_inputs(seed))
    spreads = {}
    factors = {'norm_xa_g': 8.0,
     'norm_mem_g': 8.0,
     'final_norm_g': 2.742,
     'pool_scale': 8.0,
     'hgrn_norm_g': 7.436}
    for name, (base, spread) in spreads.items():
        noise = np.random.default_rng([zlib.crc32(name.encode()), seed]).standard_normal(out[name].shape)
        drawn = base * np.exp(spread * noise) if base else spread * noise
        out[name] = __import__('jax').numpy.asarray(drawn.astype(out[name].dtype))
    for name, factor in factors.items():
        out[name] = (out[name] * factor).astype(out[name].dtype)
    return out
```

```python
from contextlib import ExitStack

import concourse.bass as bass
from concourse import mybir

ALU = mybir.AluOpType
ACT = mybir.ActivationFunctionType
AX = mybir.AxisListType
F32 = mybir.dt.float32
F32R = mybir.dt.float32r

P = 128
D = 2048
S = 256
KT = D // P
CH = 256
NP = 4
KP = KT // NP
EPS = 1e-6
HC = 32
NHC = S // HC
HEAD = 128
XA_HEADS = 4
XA_SCALE = float(D // XA_HEADS) ** -0.5
SB_SCALE = float(HEAD) ** -0.5
WIDTH = D // 2
BIG = 3.0e38
WINDOWS = (2, 4, 8, 16)
PAD = 16

PARAMS = {}
for _name, _n in (("mix0", 16), ("mix1", 16), ("xa0", 16), ("xa1", 16), ("mem0", 16), ("mem1", 16),
                  ("final", 16), ("pool_scale", 8), ("bound0", 8), ("bound1", 8), ("hgrn_g", 8)):
    PARAMS[_name] = (sum(n for _, n in PARAMS.values()), _n)
N_PARAMS = sum(n for _, n in PARAMS.values())

CONSTS = {}
for _name, _n in (("ident", P), ("ones", P), ("neg_tri", P), ("neg_ones", P), ("sb_mask", 3 * P),
                  ("hg_mask", P), ("reset", S), ("chunk_mask", P // HC)):
    CONSTS[_name] = (sum(n for _, n in CONSTS.values()), _n)
N_CONSTS = sum(n for _, n in CONSTS.values())

C_KV0, C_POOL, C_GATE, C_HGRN, C_OUT0, C_XQ0, C_OX0 = 0, 16, 20, 24, 40, 48, 56
C_KV1, C_SB, C_OUT1, C_XQ1, C_OX1, C_END = 64, 80, 112, 120, 128, 136


def build(nc, x, mem, params, consts, inv_count, pool_w, w_in_even, w_out_even, w_in_odd, w_out_odd,
          xa_wq, xa_wkv, xa_wo, out, stop=None):
    with ExitStack() as ctx:
        def sb(name, shape, dt=F32):
            return ctx.enter_context(nc.sbuf_tensor(name, shape, dt))

        def sem(name):
            return ctx.enter_context(nc.semaphore(name))

        raw = sb("raw", [P, NP, KP, CH])
        wpair = sb("wpair", [P, KT, 2, CH], F32R)
        xpair = sb("xpair", [P, KT, 2, S], F32R)
        ypair = sb("ypair", [P, KT, 2, S], F32R)
        xT = sb("xT", [P, KT, S])
        xkT = sb("xkT", [P, KT, S])
        xv = sb("xv", [P, 2, D])
        par = sb("par", [P, N_PARAMS])
        cst = sb("cst", [P, N_CONSTS])
        rs = sb("rs", [P, S + 2])
        acc = sb("acc", [P, 2, S])
        sq = sb("sq", [P, 2, S])
        tmp = sb("tmp", [P, 2, 2, S])
        small = sb("small", [P, 48])
        SCR = 8200
        scratch = sb("scratch", [P, SCR])
        ps = ctx.enter_context(nc.psum_tensor("ps", [P, 8, 512], F32))

        def prm(name, a=0, n=None):
            o, m = PARAMS[name]
            return par[:, o + a:o + a + (n or m)]

        def const(name):
            o, n = CONSTS[name]
            return cst[:, o:o + n]

        def view(off, *shape):
            n = 1
            for s_ in shape:
                n *= s_
            assert off + n <= SCR
            v = scratch[:, off:off + n]
            if len(shape) == 2:
                v = v.rearrange("p (a b) -> p a b", a=shape[0])
            if len(shape) == 3:
                v = v.rearrange("p (a b c) -> p a b c", a=shape[0], b=shape[1])
            return v

        ident, ones = const("ident"), const("ones")
        rs_row = rs[:, 0:S]
        rs_row2 = rs_row.unsqueeze(1).to_broadcast([P, 2, S])
        rs_col = rs[:, S:S + 2]
        rs_col2 = rs_col.unsqueeze(2).to_broadcast([P, 2, S])
        mem_ss, mem_rs = small[:, 0:2], small[:, 2:4]
        eps = small[:, 10:11]
        xa_negmax, xa_sum, xa_rsum = small[:, 4:6], small[:, 6:8], small[:, 8:10]
        lb, oml = small[:, 16:24], small[:, 24:32]
        lb_t0, lb_t1 = small[:, 32:40], small[:, 40:48]

        x_nat, junk = view(0, 2, D), view(4096, D)
        pool_u, pool_cs = view(0, 8, S), view(2048, 8, PAD + S)
        pool_inv, pool_wt, pool_sig = view(4224, 4, S), view(5248, 4, 2, S), view(7296, 2, S)
        hg_bd = view(0, 2, 4, CH)
        hg_k, hg_b, hg_sg = view(0, 2, S), view(512, 2, S), view(1024, 2, S)
        hg_ke, hg_eb, hg_kt = view(2048, 2, S), view(2560, 2, S), view(3072, 2, S)
        hg_q, hg_ken, hg_i = view(3584, 2, S), view(4096, 4, P), view(4608, 2, S)
        hg_sc, hg_o, hg_sq = view(4096, 4, P), view(5120, 2, S), view(5632, 2, S)
        hg_st = view(6144, 2, NHC - 1, P)
        out_xg = view(7168, 2, S)
        xq_q, xq_e, xq_pt, xq_v = view(0, 4, S), view(1024, 2, S), view(1536, 2, S), view(2048, 2, 512)
        sb_q, sb_k, sb_v, sb_sg = view(0, 2, S), view(512, 2, S), view(1024, 2, S), view(1536, 2, S)
        sb_l, sb_sp, sb_a = view(2048, 2, 3 * P), view(2816, 2, 3 * P), view(3584, 2, 3 * P)

        const_in, mem_in, x_in, pool_in, out_done = (sem(n) for n in ("const_in", "mem_in", "x_in", "pool_in", "out_done"))
        raw_in = [sem(f"raw_in{p}") for p in range(NP)]
        hi_ready = sem("hi_ready")
        lo_ready = sem("lo_ready")
        piece_done = sem("piece_done")
        evac_done = sem("evac_done")
        xpair_ready = sem("xpair_ready")
        ypair_ready = sem("ypair_ready")
        names = """mem_squares mem_scale mem_normed tr_done tr_hi xt_copied xt_done eps_ready acc_ready acc_zero stats_done rs_raw rs_inverse rs_ready mem_inverse
            lb_a lb_b lb_c lb_d lb_ready prod_ready cs_ready diff_ready diff_scaled mixed_ready pool_g pool_sig_ready pool_gs pool_mm pool_y
            y_hi hg_logit hg_sig hg_f0 hg_f1 hg_logf hg_bcum hg_exps hg_d hg_kexp hg_keys hg_ktr hg_kcopy hg_values hg_bd_ready
            hg_u hg_state hg_query hg_scores hg_scores_m hg_omm hg_osq hg_norm hg_r0 hg_r1 hg_gate hg_gsig hg_gg0 hg_gg1 hg_y0 hg_y1
            out_tmp x_new x_sq xg_ready xg_hi
            xa_q xa_vcopy xa_scores xa_max xa_exp xa_rs xa_p xa_ptr xa_pt xa_pv xa_hi
            sb_qr sb_kr sb_z sb_abs sb_exp sb_ln sb_sp0 sb_sp1 sb_cum sb_aexp sb_am sb_vr sb_av sb_gate sb_gsig sb_gg sb_y
            fin_tr fin_out0 fin_out1 cs_zero""".split()
        s = {n: sem(n) for n in names}

        block = ctx.enter_context(nc.Block())

        def wview(w):
            return w.rearrange("(k p) n -> p k n", p=P)

        W_ine, W_oute, W_ino, W_outo = (wview(w[0]) for w in (w_in_even, w_out_even, w_in_odd, w_out_odd))
        W_q, W_kv, W_o = ([wview(w[l]) for l in range(2)] for w in (xa_wq, xa_wkv, xa_wo))

        @block.sync
        def _(sp):
            def load_chunk(c, w, col):
                for p in range(NP):
                    sp.wait_ge(lo_ready, c * 4 + (p + 1))
                    sp.dma_start(raw[:, p], w[:, KP * p:KP * (p + 1), bass.ds(col, CH)]).then_inc(raw_in[p], 16)

            def plain(c0, w, n_chunks):
                with sp.Fori(0, n_chunks // 2, 1) as it:
                    for j in range(2):
                        load_chunk(it * 2 + (c0 + j), w, it * (2 * CH) + j * CH)

            mem_v = mem[0].rearrange("(r p) d -> p r d", p=P)
            sp.dma_start(xv[:], mem_v).then_inc(mem_in, 16)
            sp.dma_start(par[:], params).then_inc(const_in, 16)
            sp.dma_start(cst[:], consts).then_inc(const_in, 16)
            sp.dma_start(x_nat, x[0].rearrange("(r p) d -> p r d", p=P)).then_inc(x_in, 16)
            plain(C_KV0, W_kv[0], 16)
            sp.wait_ge(s["tr_done"], 16)
            sp.dma_start(pool_inv, inv_count).then_inc(pool_in, 16)
            sp.dma_start(pool_wt, pool_w[0].rearrange("g (t p) d -> p (g t) d", p=P)).then_inc(pool_in, 16)
            plain(C_POOL, W_ine, 8)
            with sp.Fori(0, 4, 1) as it:
                for j, base in enumerate((3, 4, 2, 5)):
                    load_chunk(it * 4 + (C_HGRN + j), W_ine, it * CH + base * WIDTH)
            plain(C_OUT0, W_oute, 8)
            plain(C_XQ0, W_q[0], 8)
            plain(C_OX0, W_o[0], 8)
            sp.wait_ge(s["xa_pv"], XA_HEADS)
            sp.dma_start(xv[:], mem_v).then_inc(mem_in, 16)
            plain(C_KV1, W_kv[1], 16)
            with sp.Fori(0, 8, 1) as it:
                for j in range(4):
                    load_chunk(it * 4 + (C_SB + j), W_ino, it * CH + j * D)
            plain(C_OUT1, W_outo, 8)
            plain(C_XQ1, W_q[1], 8)
            plain(C_OX1, W_o[1], 8)
            for r in range(2):
                sp.wait_ge(s[f"fin_out{r}"], 4)
                sp.dma_start(out[0, r * P:(r + 1) * P, :], xv[:, r, :]).then_inc(out_done, 16)
            sp.wait_ge(out_done, 32)

        @block.tensor
        def _(pe):
            mm, tr = nc.tensor.matmul, nc.tensor.transpose

            def piece(c, parity, p, operand, mode, ready=None):
                if p == 0:
                    pe.wait_ge(evac_done, c + 1)
                pe.wait_ge(lo_ready, c * 4 + (p + 5))
                if ready is not None:
                    pe.wait_ge(ready[0], ready[1] + 2 * (p + 1))
                for j in range(2):
                    bank = ps[:, 2 * parity + j, :]
                    for k in range(KP * p, KP * (p + 1)):
                        tile = slice(j * P, (j + 1) * P)
                        still, move = (wpair, operand) if mode == "T" else (operand, wpair)
                        mm(bank, still[:, k, 0, tile], move[:, k].rearrange("p h n -> p (h n)"),
                           start=(k == 0), stop=False)
                        last = mm(bank[:, S:2 * S], still[:, k, 1, tile], move[:, k, 0],
                                  start=False, stop=(k == KT - 1))
                last.then_inc(piece_done, 1)

            def chunk(c, parity, operand, mode, ready=None, hooks=()):
                for p in range(NP):
                    piece(c, parity, p, operand, mode, ready)
                    for at, work in hooks:
                        if at == p:
                            work()

            def transposes(src, base):
                for b in range(8):
                    if b >= 4:
                        pe.wait_ge(base[0], base[1] + b - 3)
                    for kk in range(2):
                        for r in range(2):
                            k = 2 * b + kk
                            last = tr(ps[:, 4 + b % 4, kk * S + r * P:kk * S + (r + 1) * P],
                                      src[:, r, k * P:(k + 1) * P], ident)
                    last.then_inc(s["tr_done"], 1)

            def stats(n):
                pe.wait_ge(s["acc_ready"], n)
                bank = ps[:, 7, :]
                for b in range(2):
                    mm(bank[:, 0:S], ones, acc[:, b, :], start=(b == 0), stop=False, skip_group_check=True)
                for r in range(2):
                    for b in range(2):
                        last = mm(bank[:, S + r:S + r + 1], acc[:, b, r * P:(r + 1) * P], ones[:, 0:1],
                                  start=False, stop=(r == 1 and b == 1), skip_group_check=True)
                last.then_inc(s["stats_done"], 1)

            def kv(c0):
                with pe.Fori(0, 4, 1) as it:
                    for j in range(2):
                        chunk(it * 2 + (c0 + j), j, ypair, "T")
                with pe.Fori(4, 8, 1) as it:
                    for j in range(2):
                        chunk(it * 2 + (c0 + j), j, ypair, "N")

            def out_stage(c0, ready, heads=None):
                if heads is None:
                    first = 0
                else:
                    first = 1
                    xa_scores(heads, XA_HEADS - 1, c0, ready)
                    chunk(c0 + 1, 1, ypair, "T")
                with pe.Fori(first, 4, 1) as it:
                    for j in range(2):
                        chunk(it * 2 + (c0 + j), j, ypair, "T", ready if (heads is None and j == 0) else None)

            def xa_scores(base, h, c, ready, operand=None):
                operand = ypair if operand is None else operand
                piece(c, 0, 0, operand, "T", ready)
                n = h + (base + 1)
                pe.wait_ge(s["xa_q"], n * 2)
                pe.wait_ge(ypair_ready, h * 2 + (40 if base else 16))
                for r in range(2):
                    for k in range(4):
                        last = mm(ps[:, 4, r * S:(r + 1) * S], xq_q[:, k, r * P:(r + 1) * P],
                                  xkT[:, bass.ds(h * 4 + k, 1), :].rearrange("p a b -> p (a b)"),
                                  start=(k == 0), stop=(k == 3), skip_group_check=True)
                last.then_inc(s["xa_scores"], 1)
                piece(c, 0, 1, operand, "T", ready)
                pe.wait_ge(s["xa_p"], n)
                for m in range(2):
                    for r in range(2):
                        last = tr(ps[:, 5, m * S + r * P:m * S + (r + 1) * P], xq_e[:, r, m * P:(m + 1) * P], ident)
                last.then_inc(s["xa_ptr"], 1)
                piece(c, 0, 2, operand, "T", ready)
                pe.wait_ge(s["xa_pt"], n)
                pe.wait_ge(s["xa_vcopy"], n)
                for b in range(4):
                    for m in range(2):
                        last = mm(ps[:, 6 + b // 2, (b % 2) * S:(b % 2 + 1) * S],
                                  xq_v[:, m, b * P:(b + 1) * P], xq_pt[:, m, :],
                                  start=(m == 0), stop=(m == 1), skip_group_check=True)
                last.then_inc(s["xa_pv"], 1)
                piece(c, 0, 3, operand, "T", ready)

            def xq_stage(c0, base, x_ready, n_stats):
                chunk(c0, 0, xpair, "T", x_ready, hooks=((1, lambda: stats(n_stats)),))
                chunk(c0 + 1, 1, xpair, "T")
                with pe.Fori(1, XA_HEADS, 1) as it:
                    xa_scores(base, it - 1, it * 2 + c0, None, xpair)
                    chunk(it * 2 + (c0 + 1), 1, xpair, "T")

            pe.nop().then_inc(piece_done, 4)
            pe.wait_ge(const_in, 32)
            pe.wait_ge(s["mem_normed"], 2)
            transposes(xv, (ypair_ready, 0))
            pe.wait_ge(x_in, 16)
            pe.wait_ge(ypair_ready, 8)
            transposes(x_nat, (xpair_ready, 0))
            pe.wait_ge(xpair_ready, 8)
            stats(1)
            kv(C_KV0)
            for c in range(C_POOL, C_GATE):
                chunk(c, c % 2, xpair, "T")

            def pool_product(g):
                def work():
                    pe.wait_ge(pool_in, 32)
                    pe.wait_ge(s["mixed_ready"], g + 1)
                    if g >= 2:
                        pe.wait_ge(s["pool_y"], 2 * (g - 1))
                    for b in range(2):
                        for t in range(2):
                            last = mm(ps[:, 4 + g % 2, b * S:(b + 1) * S], pool_wt[:, g, t, b * P:(b + 1) * P],
                                      pool_u[:, 2 * g + t, :], start=(t == 0), stop=(t == 1), skip_group_check=True)
                    last.then_inc(s["pool_mm"], 1)
                return work

            for g in range(4):
                chunk(C_GATE + g, g % 2, xpair, "T", hooks=((3, pool_product(g)),))

            with pe.Fori(0, 4, 1) as it:
                def key_transposes():
                    pe.wait_ge(s["hg_keys"], it + 1)
                    for a in range(4):
                        last = tr(ps[:, 4, a * P:(a + 1) * P], hg_ke[:, a // 2, (a % 2) * P:(a % 2 + 1) * P], ident)
                    last.then_inc(s["hg_ktr"], 1)

                def chunk_updates():
                    pe.wait_ge(s["hg_kcopy"], it + 1)
                    pe.wait_ge(s["hg_bd_ready"], it + 1)
                    for a in range(4):
                        h, t = a // 2, a % 2
                        last = mm(ps[:, 4 + a, :], hg_ken[:, a, :], hg_bd[:, t, :, h * P:(h + 1) * P],
                                  start=True, stop=True)
                    last.then_inc(s["hg_u"], 1)

                def intra_scores():
                    pe.wait_ge(s["hg_query"], it + 1)
                    for a in range(4):
                        t = slice((a % 2) * P, (a % 2 + 1) * P)
                        last = mm(ps[:, 4, a * P:(a + 1) * P], hg_kt[:, a // 2, t], hg_q[:, a // 2, t],
                                  start=True, stop=True, skip_group_check=True)
                    last.then_inc(s["hg_scores"], 1)

                def outputs():
                    pe.wait_ge(s["hg_scores_m"], it + 1)
                    for h in range(2):
                        for t in range(2):
                            mm(ps[:, 5, h * S + t * P:h * S + (t + 1) * P], hg_i[:, t, h * P:(h + 1) * P],
                               hg_sc[:, 2 * h + t, :], start=(h == 0 and t == 0), stop=False, skip_group_check=True)
                        for n in range(1, NHC):
                            last = mm(ps[:, 5, h * S + n * HC:h * S + (n + 1) * HC], hg_st[:, h, n - 1, :],
                                      hg_q[:, h, n * HC:(n + 1) * HC], start=False,
                                      stop=(h == 1 and n == NHC - 1), skip_group_check=True)
                    last.then_inc(s["hg_omm"], 1)

                def head_norm():
                    pe.wait_ge(s["hg_osq"], it + 1)
                    mm(ps[:, 6, :], ones, hg_sq.rearrange("p a b -> p (a b)"),
                       start=True, stop=True).then_inc(s["hg_norm"], 1)

                c = it * 4 + C_HGRN
                chunk(c, 0, xpair, "T")
                chunk(c + 1, 1, xpair, "N")
                chunk(c + 2, 0, xpair, "T", hooks=((0, key_transposes), (2, chunk_updates)))
                chunk(c + 3, 1, xpair, "T", hooks=((0, intra_scores), (2, outputs), (3, head_norm)))

            out_stage(C_OUT0, (ypair_ready, 8))
            xq_stage(C_XQ0, 0, (xpair_ready, 8), 2)
            out_stage(C_OX0, (ypair_ready, 16), heads=0)
            stats(3)
            pe.wait_ge(s["mem_normed"], 4)
            pe.wait_ge(s["rs_raw"], 3)
            transposes(xv, (ypair_ready, 24))
            with pe.Fori(0, 4, 1) as it:
                for j in range(2):
                    chunk(it * 2 + (C_KV1 + j), j, ypair, "T", (ypair_ready, 24) if j == 0 else None)
            with pe.Fori(4, 8, 1) as it:
                for j in range(2):
                    chunk(it * 2 + (C_KV1 + j), j, ypair, "N")

            with pe.Fori(0, 8, 1) as it:
                def logits():
                    pe.wait_ge(s["sb_kr"], it + 1)
                    for h in range(2):
                        mm(ps[:, 4 + h, 0:S], sb_k[:, h, 0:P], sb_q[:, h, :],
                           start=True, stop=False, skip_group_check=True)
                        mm(ps[:, 4 + h, S:S + P], sb_k[:, h, P:S], sb_q[:, h, P:S],
                           start=False, stop=False, skip_group_check=True).then_inc(s["sb_z"], 1)

                def cumulate():
                    for h in range(2):
                        pe.wait_ge(s["sb_sp1"], it * 2 + (h + 1))
                        bank = ps[:, 4 + h, :]
                        mm(bank[:, 0:S], const("neg_tri"), sb_sp[:, h, 0:S], start=False, stop=False, skip_group_check=True)
                        mm(bank[:, P:S], const("neg_ones"), sb_sp[:, h, S:S + P], start=False, stop=False, skip_group_check=True)
                        mm(bank[:, S:S + P], const("neg_tri"), sb_sp[:, h, S:S + P], start=False, stop=True,
                           skip_group_check=True).then_inc(s["sb_cum"], 1)

                def mix_values():
                    pe.wait_ge(s["sb_vr"], it + 1)
                    pe.wait_ge(s["sb_am"], it * 2 + 2)
                    for h in range(2):
                        v = slice(h * P, (h + 1) * P)
                        mm(ps[:, 6, h * S:(h + 1) * S], sb_v[:, 0, v], sb_a[:, h, 0:S],
                           start=(h == 0), stop=False, skip_group_check=True)
                        last = mm(ps[:, 6, h * S + P:(h + 1) * S], sb_v[:, 1, v], sb_a[:, h, S:S + P],
                                  start=False, stop=(h == 1), skip_group_check=True)
                    last.then_inc(s["sb_av"], 1)

                c = it * 4 + C_SB
                chunk(c, 0, xpair, "T", (xpair_ready, 16))
                chunk(c + 1, 1, xpair, "T")
                chunk(c + 2, 0, xpair, "N", hooks=((0, logits), (2, cumulate)))
                chunk(c + 3, 1, xpair, "T", hooks=((1, mix_values),))

            out_stage(C_OUT1, (ypair_ready, 32))
            xq_stage(C_XQ1, XA_HEADS, (xpair_ready, 24), 4)
            out_stage(C_OX1, (ypair_ready, 40), heads=XA_HEADS)
            stats(5)
            pe.wait_ge(s["rs_raw"], 5)
            pe.wait_ge(evac_done, C_END + 2)
            for r in range(2):
                for q in range(4):
                    for k in range(4 * q, 4 * q + 4):
                        last = tr(ps[:, 4 * r + q, (k % 4) * P:(k % 4 + 1) * P], xkT[:, k, r * P:(r + 1) * P], ident)
                    last.then_inc(s["fin_tr"], 1)

        @block.scalar
        def _(act):
            fn = nc.scalar.activation

            def split_hi(c, p):
                act.wait_ge(raw_in[p], c * 16 + 16)
                act.wait_ge(piece_done, c * 4 + (p + 1))
                fn(wpair[:, KP * p:KP * (p + 1), 0, :], raw[:, p], ACT.Copy).then_inc(hi_ready, 1)

            def slot(c, steps=(), convert=True):
                for p in range(NP):
                    if convert:
                        split_hi(c + 1, p)
                    for at, work in steps:
                        if at == p:
                            work()

            def rs_root(n):
                act.wait_ge(s["rs_inverse"], n)
                fn(rs[:, :], rs[:, :], ACT.Sqrt).then_inc(s["rs_ready"], 1)

            def transposed_mem(gain, tr0):
                for b in range(8):
                    act.wait_ge(s["tr_done"], tr0 + b + 1)
                    for kk in range(2):
                        last = fn(ypair[:, 2 * b + kk, 0, :], ps[:, 4 + b % 4, kk * S:(kk + 1) * S], ACT.Copy,
                                  scale=prm(gain, 2 * b + kk, 1))
                    last.then_inc(s["tr_hi"], 1)

            def out_stage(c0, heads=None, pair=True):
                def hi(c, it, j):
                    def work():
                        act.wait_ge(s["xg_ready"], n_xg + it * 2 + (j + 1))
                        k = it * 4 + 2 * j
                        fn(xpair[:, bass.ds(k, 2), 0, :], out_xg, ACT.Copy).then_inc(s["xg_hi"], 1)
                    return work
                n_xg = xg_count[0]
                xg_count[0] += 8
                first = 0
                if heads is not None:
                    slot(c0, attend(heads, XA_HEADS - 1) + (((3, hi(c0, 0, 0)),) if pair else ()))
                    slot(c0 + 1, ((3, hi(c0, 0, 1)),) if pair else ())
                    first = 1
                last_it = 3 if c0 == C_OX1 else 4
                with act.Fori(first, last_it, 1) as it:
                    for j in range(2):
                        slot(it * 2 + (c0 + j), ((3, hi(c0, it, j)),) if pair else ())
                if c0 == C_OX1:
                    slot(C_END - 2)
                    slot(C_END - 1, convert=False)

            xg_count = [0]

            def attend(base, h):
                n = h + (base + 1)

                def exps():
                    act.wait_ge(s["xa_max"], n)
                    for r in range(2):
                        last = fn(xq_e[:, r, :], ps[:, 4, r * S:(r + 1) * S], ACT.Exp,
                                  bias=xa_negmax[:, r:r + 1], accum_out=xa_sum[:, r:r + 1])
                    last.then_inc(s["xa_exp"], 1)

                def copy_pt():
                    act.wait_ge(s["xa_ptr"], n)
                    fn(xq_pt.rearrange("p a b -> p (a b)"), ps[:, 5, :], ACT.Copy).then_inc(s["xa_pt"], 1)

                def hi():
                    act.wait_ge(s["xa_pv"], n)
                    for b in range(2):
                        fn(ypair[:, bass.ds(h * 4 + 2 * b, 2), 0, :],
                           ps[:, 6 + b, :].rearrange("p (a b) -> p a b", a=2), ACT.Copy).then_inc(s["xa_hi"], 1)
                return ((0, exps), (1, copy_pt), (2, hi))

            def xq_stage(c0, base, n_stats):
                slot(c0, ((2, lambda: rs_root(n_stats)),))
                slot(c0 + 1)
                with act.Fori(1, XA_HEADS, 1) as it:
                    slot(it * 2 + c0, attend(base, it - 1))
                    slot(it * 2 + (c0 + 1))

            act.wait_ge(s["eps_ready"], 1)
            act.wait_ge(mem_in, 16)
            for r in range(2):
                if r:
                    act.wait_ge(s["mem_squares"], 1)
                fn(junk, xv[:, r, :], ACT.Square, accum_out=mem_ss[:, r:r + 1]).then_inc(s["mem_squares"], 1)
            act.wait_ge(s["mem_inverse"], 1)
            fn(mem_rs, mem_rs, ACT.Sqrt).then_inc(s["mem_scale"], 1)
            act.wait_ge(s["lb_a"], 2)
            fn(lb_t0, lb_t0, ACT.Exp)
            fn(lb_t1, lb_t1, ACT.Exp).then_inc(s["lb_b"], 1)
            for p in range(NP):
                split_hi(0, p)
            transposed_mem("mem0", 0)
            for b in range(8):
                act.wait_ge(s["tr_done"], 8 + b + 1)
                fn(xT[:, 2 * b:2 * b + 2, :], ps[:, 4 + b % 4, :].rearrange("p (a b) -> p a b", a=2),
                   ACT.Copy).then_inc(s["xt_copied"], 1)
                for kk in range(2):
                    last = fn(xpair[:, 2 * b + kk, 0, :], ps[:, 4 + b % 4, kk * S:(kk + 1) * S], ACT.Copy,
                              scale=prm("mix0", 2 * b + kk, 1))
                last.then_inc(s["tr_hi"], 1)
            rs_root(1)
            with act.Fori(0, C_POOL // 2, 1) as it:
                for j in range(2):
                    slot(it * 2 + j)
            for c in range(C_POOL, C_GATE):
                slot(c)
            for g in range(4):
                def gate_sigmoid():
                    act.wait_ge(s["pool_g"], g + 1)
                    fn(pool_sig, tmp[:, g % 2], ACT.Sigmoid).then_inc(s["pool_sig_ready"], 1)
                    act.wait_ge(s["pool_y"], 2 * (g + 1))
                    fn(ypair[:, 2 * g:2 * g + 2, 0, :], tmp[:, g % 2], ACT.Copy).then_inc(s["y_hi"], 1)
                slot(C_GATE + g, ((3, gate_sigmoid),))

            with act.Fori(0, 4, 1) as it:
                def sigmoid():
                    act.wait_ge(s["hg_logit"], it + 1)
                    fn(hg_k, hg_k, ACT.Sigmoid).then_inc(s["hg_sig"], 1)

                def log_f():
                    act.wait_ge(s["hg_f1"], it + 1)
                    fn(hg_ke, hg_k, ACT.Ln).then_inc(s["hg_logf"], 1)

                def exps():
                    act.wait_ge(s["hg_bcum"], it + 1)
                    fn(hg_eb, hg_b, ACT.Exp)
                    fn(hg_kt, hg_b, ACT.Exp, scale=-1.0).then_inc(s["hg_exps"], 1)

                def key_exp():
                    act.wait_ge(s["hg_d"], it + 1)
                    fn(hg_ke, hg_ke, ACT.Exp).then_inc(s["hg_kexp"], 1)

                def key_copy():
                    act.wait_ge(s["hg_ktr"], it + 1)
                    fn(hg_ken.rearrange("p a b -> p (a b)"), ps[:, 4, :], ACT.Copy).then_inc(s["hg_kcopy"], 1)

                def squares():
                    act.wait_ge(s["hg_omm"], it + 1)
                    o = ps[:, 5, :].rearrange("p (a b) -> p a b", a=2)
                    fn(hg_sq, o, ACT.Square)
                    fn(hg_o, o, ACT.Copy).then_inc(s["hg_osq"], 1)

                def norm_factor():
                    act.wait_ge(s["hg_norm"], it + 1)
                    fn(hg_ke, ps[:, 6, :].rearrange("p (a b) -> p a b", a=2), ACT.Ln, scale=1.0 / HEAD,
                       bias=eps).then_inc(s["hg_r0"], 1)
                    act.wait_ge(s["hg_r0"], it + 1)
                    fn(hg_ke, hg_ke, ACT.Exp, scale=-0.5).then_inc(s["hg_r1"], 1)

                def gate():
                    act.wait_ge(s["hg_gate"], it + 1)
                    fn(hg_sg, tmp[:, 1], ACT.Sigmoid).then_inc(s["hg_gsig"], 1)
                    act.wait_ge(s["hg_y1"], it + 1)
                    fn(ypair[:, bass.ds(it * 2 + 8, 2), 0, :], hg_o, ACT.Copy).then_inc(s["y_hi"], 1)

                c = it * 4 + C_HGRN
                slot(c, ((3, sigmoid),))
                slot(c + 1, ((0, log_f), (1, exps), (2, key_exp)))
                slot(c + 2, ((1, key_copy),))
                slot(c + 3, ((3, squares), (3, norm_factor), (3, gate)))

            out_stage(C_OUT0)
            xq_stage(C_XQ0, 0, 2)
            out_stage(C_OX0, heads=0)
            rs_root(3)
            transposed_mem("mem1", 16)
            with act.Fori(0, 8, 1) as it:
                for j in range(2):
                    slot(it * 2 + (C_KV1 + j))

            with act.Fori(0, 8, 1) as it:
                def softplus():
                    for h in range(2):
                        act.wait_ge(s["sb_z"], it * 2 + (h + 1))
                        fn(sb_l[:, h, :], ps[:, 4 + h, 0:3 * P], ACT.Abs).then_inc(s["sb_abs"], 1)
                    for h in range(2):
                        act.wait_ge(s["sb_abs"], it * 2 + (h + 1))
                        fn(sb_l[:, h, :], sb_l[:, h, :], ACT.Exp, scale=-1.0).then_inc(s["sb_exp"], 1)
                    for h in range(2):
                        act.wait_ge(s["sb_exp"], it * 2 + (h + 1))
                        fn(sb_l[:, h, :], sb_l[:, h, :], ACT.Ln, bias=1.0).then_inc(s["sb_ln"], 1)

                def weights():
                    for h in range(2):
                        act.wait_ge(s["sb_cum"], it * 2 + (h + 1))
                        fn(sb_a[:, h, :], ps[:, 4 + h, 0:3 * P], ACT.Exp).then_inc(s["sb_aexp"], 1)

                def gate():
                    act.wait_ge(s["sb_gate"], it + 1)
                    fn(sb_sg, tmp[:, 1], ACT.Sigmoid).then_inc(s["sb_gsig"], 1)
                    act.wait_ge(s["sb_y"], it + 1)
                    fn(ypair[:, bass.ds(it * 2, 2), 0, :], tmp[:, 1], ACT.Copy).then_inc(s["y_hi"], 1)

                c = it * 4 + C_SB
                slot(c)
                slot(c + 1)
                slot(c + 2, ((1, softplus), (3, weights)))
                slot(c + 3, ((3, gate),))

            out_stage(C_OUT1)
            xq_stage(C_XQ1, XA_HEADS, 4)
            out_stage(C_OX1, heads=XA_HEADS, pair=False)
            rs_root(5)
            act.wait_ge(s["rs_ready"], 5)
            for n in range(0, 8, 2):
                act.wait_ge(s["fin_tr"], n + 1)
                fn(xv[:, n // 4, (n % 4) * 512:(n % 4 + 1) * 512], ps[:, n, :], ACT.Copy,
                   scale=rs[:, S + n // 4:S + n // 4 + 1]).then_inc(s[f"fin_out{n // 4}"], 1)

        @block.vector
        def _(dve):
            v = nc.vector

            def split_lo(c, p):
                dve.wait_ge(hi_ready, c * 4 + (p + 1))
                kp = slice(KP * p, KP * (p + 1))
                v.tensor_tensor(wpair[:, kp, 1, :], raw[:, p], wpair[:, kp, 0, :].bitcast(F32),
                                ALU.subtract).then_inc(lo_ready, 1)

            def slot(c, steps=(), convert=True):
                for p in range(NP):
                    if convert:
                        split_lo(c + 1, p)
                    for at, work in steps:
                        if at == p:
                            work()

            def take(c, parity, dst):
                dve.wait_ge(piece_done, c * 4 + 8)
                v.tensor_reduce(dst, ps[:, 2 * parity:2 * parity + 2, :].rearrange("p j (h n) -> p j n h", h=2),
                                AX.X, ALU.add).then_inc(evac_done, 1)
                dve.wait_ge(evac_done, c + 3)

            def rs_step(n):
                dve.wait_ge(s["stats_done"], n)
                v.tensor_scalar(rs[:, :], ps[:, 7, 0:S + 2], 1.0 / D, EPS, ALU.mult, ALU.add).then_inc(s["rs_raw"], 1)
                dve.wait_ge(s["rs_raw"], n)
                v.reciprocal(rs[:, :], rs[:, :]).then_inc(s["rs_inverse"], 1)
                dve.wait_ge(s["rs_ready"], n)

            def transposed_lo(dst, gain, hi0, done):
                for b in range(8):
                    dve.wait_ge(s["tr_hi"], hi0 + b + 1)
                    for kk in range(2):
                        k = 2 * b + kk
                        last = v.scalar_tensor_tensor(dst[:, k, 1, :], ps[:, 4 + b % 4, kk * S:(kk + 1) * S],
                                                      prm(gain, k, 1), dst[:, k, 0, :].bitcast(F32),
                                                      ALU.mult, ALU.subtract)
                    last.then_inc(done, 1)

            def kv(c0):
                with dve.Fori(0, 4, 1) as it:
                    for j in range(2):
                        def keys():
                            take(it * 2 + (c0 + j), j, xkT[:, bass.ds(it * 4 + 2 * j, 2), :])
                        slot(it * 2 + (c0 + j), ((3, keys),))
                with dve.Fori(0, 4, 1) as it:
                    for j in range(2):
                        def values():
                            take(it * 2 + (c0 + 8 + j), j, xv[:, :, bass.ds(it * (2 * CH) + j * CH, CH)])
                        slot(it * 2 + (c0 + 8 + j), ((3, values),))

            def attend(base, h):
                n = h + (base + 1)

                def softmax():
                    dve.wait_ge(s["xa_scores"], n)
                    v.tensor_reduce(xa_negmax, ps[:, 4, :].rearrange("p (a b) -> p a b", a=2), AX.X, ALU.max,
                                    negate=True).then_inc(s["xa_max"], 1)
                    dve.wait_ge(s["xa_exp"], n)
                    v.reciprocal(xa_rsum, xa_sum).then_inc(s["xa_rs"], 1)
                    dve.wait_ge(s["xa_rs"], n)
                    for r in range(2):
                        last = v.tensor_scalar(xq_e[:, r, :], xq_e[:, r, :], xa_rsum[:, r:r + 1], None, ALU.mult)
                    last.then_inc(s["xa_p"], 1)

                def lo():
                    for b in range(2):
                        dve.wait_ge(s["xa_hi"], n * 2 + (b - 1))
                        v.tensor_tensor(ypair[:, bass.ds(h * 4 + 2 * b, 2), 1, :],
                                        ps[:, 6 + b, :].rearrange("p (a b) -> p a b", a=2),
                                        ypair[:, bass.ds(h * 4 + 2 * b, 2), 0, :].bitcast(F32),
                                        ALU.subtract).then_inc(ypair_ready, 1)
                return ((0, softmax), (2, lo))

            def xq_stage(c0, base, n_stats):
                def query(it, j):
                    def work():
                        take(it * 2 + (c0 + j), j, tmp[:, j])
                        v.scalar_tensor_tensor(xq_q[:, 2 * j:2 * j + 2, :], tmp[:, j], XA_SCALE, rs_row2,
                                               ALU.mult, ALU.mult).then_inc(s["xa_q"], 1)
                    return work
                slot(c0, ((2, lambda: rs_step(n_stats)), (3, query(0, 0))))
                slot(c0 + 1, ((3, query(0, 1)),))
                with dve.Fori(1, XA_HEADS, 1) as it:
                    slot(it * 2 + c0, attend(base, it - 1) + ((3, query(it, 0)),))
                    slot(it * 2 + (c0 + 1), ((3, query(it, 1)),))

            out_count = [0]

            def out_stage(c0, heads=None, pair=True):
                n0 = out_count[0]
                out_count[0] += 8

                def residual(it, j):
                    def work():
                        if not pair:
                            dve.wait_ge(s["x_new"], n0 + it * 2 + (j - 1))
                        take(it * 2 + (c0 + j), j, tmp[:, j])
                        v.nop().then_inc(s["out_tmp"], 1)
                        if pair:
                            dve.wait_ge(s["xg_hi"], n0 + it * 2 + (j + 1))
                            v.tensor_tensor(xpair[:, bass.ds(it * 4 + 2 * j, 2), 1, :], out_xg,
                                            xpair[:, bass.ds(it * 4 + 2 * j, 2), 0, :].bitcast(F32),
                                            ALU.subtract).then_inc(xpair_ready, 1)
                    return work
                first = 0
                if heads is not None:
                    slot(c0, attend(heads, XA_HEADS - 1) + ((3, residual(0, 0)),))
                    slot(c0 + 1, ((3, residual(0, 1)),))
                    first = 1
                last_it = 3 if c0 == C_OX1 else 4
                with dve.Fori(first, last_it, 1) as it:
                    for j in range(2):
                        slot(it * 2 + (c0 + j), ((3, residual(it, j)),))
                if c0 == C_OX1:
                    slot(C_END - 2, ((3, residual(3, 0)),))
                    slot(C_END - 1, ((3, residual(3, 1)),), convert=False)

            v.memset(eps, EPS).then_inc(s["eps_ready"], 1)
            v.nop().then_inc(lo_ready, 4)
            v.nop().then_inc(evac_done, 2)
            dve.wait_ge(const_in, 32)
            v.tensor_tensor(lb, prm("bound0"), prm("bound1"), ALU.max).then_inc(s["lb_a"], 1)
            dve.wait_ge(s["lb_a"], 1)
            v.tensor_tensor(lb_t0, prm("bound0"), lb, ALU.subtract)
            v.tensor_tensor(lb_t1, prm("bound1"), lb, ALU.subtract).then_inc(s["lb_a"], 1)
            dve.wait_ge(s["mem_squares"], 2)
            v.tensor_scalar(mem_rs, mem_ss, 1.0 / D, EPS, ALU.mult, ALU.add).then_inc(s["mem_scale"], 1)
            dve.wait_ge(s["mem_scale"], 1)
            v.reciprocal(mem_rs, mem_rs).then_inc(s["mem_inverse"], 1)
            dve.wait_ge(s["mem_scale"], 2)
            for r in range(2):
                v.tensor_scalar(xv[:, r, :], xv[:, r, :], mem_rs[:, r:r + 1], None, ALU.mult).then_inc(s["mem_normed"], 1)
            dve.wait_ge(s["lb_b"], 1)
            v.tensor_tensor(lb_t1, lb_t0, lb_t1, ALU.add).then_inc(s["lb_c"], 1)
            dve.wait_ge(s["lb_c"], 1)
            v.reciprocal(lb_t1, lb_t1).then_inc(s["lb_c"], 1)
            dve.wait_ge(s["lb_c"], 2)
            v.tensor_tensor(lb, lb_t0, lb_t1, ALU.mult).then_inc(s["lb_d"], 1)
            dve.wait_ge(s["lb_d"], 1)
            v.tensor_scalar(oml, lb, -1.0, 1.0, ALU.mult, ALU.add).then_inc(s["lb_ready"], 1)
            for p in range(NP):
                split_lo(0, p)
            transposed_lo(ypair, "mem0", 0, ypair_ready)
            transposed_lo(xpair, "mix0", 8, xpair_ready)
            rs_step(1)
            kv(C_KV0)

            for c in range(C_POOL, C_GATE):
                def pool_input():
                    b = 2 * (c - C_POOL)
                    take(c, c % 2, tmp[:, c % 2])
                    v.tensor_tensor(pool_u[:, b:b + 2, :], tmp[:, c % 2], rs_row2, ALU.mult).then_inc(s["prod_ready"], 1)
                    dve.wait_ge(s["prod_ready"], c - C_POOL + 1)
                    if c == C_POOL:
                        dve.wait_ge(s["cs_zero"], 1)
                    for k in range(b, b + 2):
                        last = v.tensor_tensor_scan(pool_cs[:, k, PAD:], ones[:, 0:1].to_broadcast([P, S]),
                                                    pool_u[:, k, :], 0.0, ALU.mult, ALU.add)
                    last.then_inc(s["cs_ready"], 1)
                slot(c, ((3, pool_input),))
            for g in range(4):
                def pool_gate():
                    t = tmp[:, g % 2]
                    take(C_GATE + g, g % 2, t)
                    v.tensor_tensor(t, t, rs_row2, ALU.mult).then_inc(s["pool_g"], 1)
                    dve.wait_ge(s["pool_sig_ready"], g + 1)
                    v.tensor_tensor(t, t, pool_sig, ALU.mult).then_inc(s["pool_gs"], 1)
                    dve.wait_ge(s["pool_gs"], g + 1)
                    dve.wait_ge(s["pool_mm"], g + 1)
                    for b in range(2):
                        v.scalar_tensor_tensor(t[:, b, :], ps[:, 4 + g % 2, b * S:(b + 1) * S],
                                               prm("pool_scale", 2 * g + b, 1), t[:, b, :],
                                               ALU.mult, ALU.mult).then_inc(s["pool_y"], 1)
                    dve.wait_ge(s["y_hi"], g + 1)
                    v.tensor_tensor(ypair[:, 2 * g:2 * g + 2, 1, :], t, ypair[:, 2 * g:2 * g + 2, 0, :].bitcast(F32),
                                    ALU.subtract).then_inc(ypair_ready, 1)
                slot(C_GATE + g, ((3, pool_gate),))

            with dve.Fori(0, 4, 1) as it:
                c = it * 4 + C_HGRN

                def bc(ap):
                    return ap.unsqueeze(2).to_broadcast([P, 2, S])

                def logits():
                    take(c, 0, tmp[:, 0])
                    v.tensor_tensor(hg_k, tmp[:, 0], rs_row2, ALU.mult).then_inc(s["hg_logit"], 1)

                def forget():
                    dve.wait_ge(s["hg_sig"], it + 1)
                    v.tensor_tensor(hg_k, hg_k, bc(oml[:, bass.ds(it * 2, 2)]), ALU.mult).then_inc(s["hg_f0"], 1)
                    dve.wait_ge(s["hg_f0"], it + 1)
                    v.tensor_tensor(hg_k, hg_k, bc(lb[:, bass.ds(it * 2, 2)]), ALU.add).then_inc(s["hg_f1"], 1)

                def cumulate():
                    dve.wait_ge(s["hg_logf"], it + 1)
                    for h in range(2):
                        last = v.tensor_tensor_scan(hg_b[:, h, :], const("reset"), hg_ke[:, h, :], 0.0, ALU.mult, ALU.add)
                    last.then_inc(s["hg_bcum"], 1)
                    v.tensor_scalar(hg_k, hg_k, -1.0, 1.0, ALU.mult, ALU.add)

                def key_exponent():
                    b4 = hg_b.rearrange("p a (n c) -> p (a n) c", c=HC)
                    dve.wait_ge(s["hg_bcum"], it + 1)
                    v.tensor_tensor(hg_ke.rearrange("p a (n c) -> p (a n) c", c=HC),
                                    b4[:, :, HC - 1:HC].to_broadcast([P, 2 * NHC, HC]), b4,
                                    ALU.subtract).then_inc(s["hg_d"], 1)

                def keys():
                    dve.wait_ge(s["hg_kexp"], it + 1)
                    dve.wait_ge(s["hg_exps"], it + 1)
                    v.tensor_tensor(hg_kt, hg_kt, hg_k, ALU.mult)
                    v.tensor_tensor(hg_ke, hg_ke, hg_k, ALU.mult).then_inc(s["hg_keys"], 1)

                def values():
                    take(c + 1, 1, tmp[:, 1])
                    v.tensor_tensor(hg_i, tmp[:, 1], rs_col2, ALU.mult).then_inc(s["hg_values"], 1)

                def states():
                    dve.wait_ge(s["hg_u"], it + 1)
                    for n in range(NHC - 1):
                        for h in range(2):
                            u = ps[:, 4 + 2 * h + n // 4, (n % 4) * P:(n % 4 + 1) * P]
                            if n == 0:
                                v.tensor_copy(hg_st[:, h, 0, :], u).then_inc(s["hg_state"], 1)
                                continue
                            at = n * HC + HC - 1
                            dve.wait_ge(s["hg_state"], it * 14 + (2 * (n - 1) + h + 1))
                            v.scalar_tensor_tensor(hg_st[:, h, n, :], hg_st[:, h, n - 1, :], hg_eb[:, h, at:at + 1], u,
                                                   ALU.mult, ALU.add).then_inc(s["hg_state"], 1)

                def queries():
                    take(c + 2, 0, tmp[:, 0])
                    v.tensor_tensor(hg_q, tmp[:, 0], rs_row2, ALU.mult).then_inc(s["prod_ready"], 1)
                    dve.wait_ge(s["prod_ready"], it + 5)
                    v.tensor_tensor(hg_q, hg_q, hg_eb, ALU.mult).then_inc(s["hg_query"], 1)

                def mask_scores():
                    dve.wait_ge(s["hg_scores"], it + 1)
                    v.tensor_tensor(hg_sc, ps[:, 4, :].rearrange("p (a b) -> p a b", a=4),
                                    const("hg_mask").unsqueeze(1).to_broadcast([P, 4, P]), ALU.mult).then_inc(s["hg_scores_m"], 1)

                def gate():
                    take(c + 3, 1, tmp[:, 1])
                    v.tensor_tensor(tmp[:, 1], tmp[:, 1], rs_row2, ALU.mult).then_inc(s["hg_gate"], 1)
                    dve.wait_ge(s["hg_r1"], it + 1)
                    v.tensor_tensor(hg_o, hg_o, hg_ke, ALU.mult).then_inc(s["hg_y0"], 1)
                    dve.wait_ge(s["hg_y0"], it + 1)
                    dve.wait_ge(s["hg_gg1"], it + 1)
                    v.tensor_tensor(hg_o, hg_o, tmp[:, 1], ALU.mult).then_inc(s["hg_y1"], 1)
                    dve.wait_ge(s["y_hi"], it + 5)
                    v.tensor_tensor(ypair[:, bass.ds(it * 2 + 8, 2), 1, :], hg_o,
                                    ypair[:, bass.ds(it * 2 + 8, 2), 0, :].bitcast(F32), ALU.subtract).then_inc(ypair_ready, 1)

                slot(c, ((3, logits),))
                slot(c + 1, ((0, forget), (1, cumulate), (2, key_exponent), (3, keys), (3, values)))
                slot(c + 2, ((3, states), (3, queries)))
                slot(c + 3, ((1, mask_scores), (3, gate)))

            out_stage(C_OUT0)
            xq_stage(C_XQ0, 0, 2)
            out_stage(C_OX0, heads=0)
            rs_step(3)
            dve.wait_ge(mem_in, 32)
            for r in range(2):
                v.tensor_scalar(xv[:, r, :], xv[:, r, :], mem_rs[:, r:r + 1], None, ALU.mult).then_inc(s["mem_normed"], 1)
            transposed_lo(ypair, "mem1", 16, ypair_ready)
            kv(C_KV1)

            with dve.Fori(0, 8, 1) as it:
                c = it * 4 + C_SB

                def queries():
                    take(c, 0, tmp[:, 0])
                    v.scalar_tensor_tensor(sb_q, tmp[:, 0], SB_SCALE, rs_row2, ALU.mult, ALU.mult).then_inc(s["sb_qr"], 1)

                def keys():
                    take(c + 1, 1, tmp[:, 1])
                    v.tensor_tensor(sb_k, tmp[:, 1], rs_row2, ALU.mult).then_inc(s["sb_kr"], 1)

                def softplus():
                    for h in range(2):
                        dve.wait_ge(s["sb_ln"], it * 2 + (h + 1))
                        v.scalar_tensor_tensor(sb_sp[:, h, :], ps[:, 4 + h, 0:3 * P], 0.0, sb_l[:, h, :],
                                               ALU.max, ALU.add).then_inc(s["sb_sp0"], 1)
                    for h in range(2):
                        dve.wait_ge(s["sb_sp0"], it * 2 + (h + 1))
                        v.tensor_tensor(sb_sp[:, h, :], sb_sp[:, h, :], const("sb_mask"), ALU.mult).then_inc(s["sb_sp1"], 1)

                def weights():
                    for h in range(2):
                        dve.wait_ge(s["sb_aexp"], it * 2 + (h + 1))
                        v.scalar_tensor_tensor(sb_a[:, h, :], sb_a[:, h, :], BIG, const("sb_mask"),
                                               ALU.min, ALU.mult).then_inc(s["sb_am"], 1)

                def values():
                    take(c + 2, 0, tmp[:, 0])
                    v.tensor_tensor(sb_v, tmp[:, 0], rs_col2, ALU.mult).then_inc(s["sb_vr"], 1)

                def gate():
                    t = tmp[:, 1]
                    take(c + 3, 1, t)
                    v.tensor_tensor(t, t, rs_row2, ALU.mult).then_inc(s["sb_gate"], 1)
                    dve.wait_ge(s["sb_gsig"], it + 1)
                    v.tensor_tensor(t, t, sb_sg, ALU.mult).then_inc(s["sb_gg"], 1)
                    dve.wait_ge(s["sb_gg"], it + 1)
                    dve.wait_ge(s["sb_av"], it + 1)
                    v.tensor_tensor(t, ps[:, 6, :].rearrange("p (a b) -> p a b", a=2), t, ALU.mult).then_inc(s["sb_y"], 1)
                    dve.wait_ge(s["y_hi"], it + 9)
                    v.tensor_tensor(ypair[:, bass.ds(it * 2, 2), 1, :], t,
                                    ypair[:, bass.ds(it * 2, 2), 0, :].bitcast(F32), ALU.subtract).then_inc(ypair_ready, 1)

                slot(c, ((3, queries),))
                slot(c + 1, ((3, keys),))
                slot(c + 2, ((1, softplus), (3, weights), (3, values)))
                slot(c + 3, ((3, gate),))

            out_stage(C_OUT1)
            xq_stage(C_XQ1, XA_HEADS, 4)
            out_stage(C_OX1, heads=XA_HEADS, pair=False)
            rs_step(5)
            for n in range(1, 8, 2):
                dve.wait_ge(s["fin_tr"], n + 1)
                v.tensor_scalar(xv[:, n // 4, (n % 4) * 512:(n % 4 + 1) * 512], ps[:, n, :],
                                rs[:, S + n // 4:S + n // 4 + 1], None, ALU.mult).then_inc(s[f"fin_out{n // 4}"], 1)

        @block.gpsimd
        def _(pool):
            g = nc.gpsimd
            sq_count = [0]

            def zero_acc(n):
                if n:
                    pool.wait_ge(s["stats_done"], n)
                g.memset(acc[:], 0.0).then_inc(s["acc_zero"], 1)
                pool.wait_ge(s["acc_zero"], n + 1)

            def add_squares(block_ap, it, n0, last=False):
                g.tensor_tensor(sq[:], block_ap, block_ap, ALU.mult).then_inc(s["x_sq"], 1)
                pool.wait_ge(s["x_sq"], it + (n0 + 1))
                ins = g.tensor_tensor(acc[:], acc[:], sq[:], ALU.add)
                return ins

            def out_stage(c0, gain, n_stats, n0, final=False, heads=None):
                zero_acc(n_stats - 1)

                def residual(it, j):
                    i = it * 2 + j
                    blk = bass.ds(it * 4 + 2 * j, 2)
                    pool.wait_ge(s["out_tmp"], i + (n0 + 1))
                    g.tensor_tensor(xT[:, blk, :], xT[:, blk, :], tmp[:, j], ALU.add).then_inc(s["x_new"], 1)
                    pool.wait_ge(s["x_new"], i + (n0 + 1))
                    o, _ = PARAMS[gain]
                    gb = par[:, bass.ds(it * 4 + (2 * j + o), 2)].unsqueeze(2).to_broadcast([P, 2, S])
                    dst = xkT[:, blk, :] if final else out_xg
                    g.tensor_tensor(dst, xT[:, blk, :], gb, ALU.mult).then_inc(s["xg_ready"], 1)
                    add_squares(xT[:, blk, :], i, n0 + 8).then_inc(s["xt_done"], 1)
                    pool.wait_ge(s["xt_done"], i + (n0 + 9))

                if heads is not None:
                    residual(0, 0)
                    residual(0, 1)
                with pool.Fori(0 if heads is None else 1, 4, 1) as it:
                    for j in range(2):
                        residual(it, j)
                pool.nop().then_inc(s["acc_ready"], 1)

            def copy_values(base, h):
                n = h + (base + 1)
                g.tensor_copy(xq_v, xv[:, :, bass.ds(h * 512, 512)]).then_inc(s["xa_vcopy"], 1)

            def xq_stage(base):
                copy_values(base, 0)
                with pool.Fori(1, XA_HEADS, 1) as it:
                    pool.wait_ge(s["xa_pv"], it + base)
                    copy_values(base, it)

            zero_acc(0)
            for b in range(8):
                pool.wait_ge(s["xt_copied"], b + 1)
                add_squares(xT[:, 2 * b:2 * b + 2, :], b, 0).then_inc(s["xt_done"], 1)
                pool.wait_ge(s["xt_done"], b + 1)
            pool.nop().then_inc(s["acc_ready"], 1)
            pool.wait_ge(s["tr_done"], 16)
            g.memset(pool_cs[:, :, 0:PAD], 0.0).then_inc(s["cs_zero"], 1)
            pool.wait_ge(pool_in, 32)
            for n in range(4):
                pool.wait_ge(s["cs_ready"], n + 1)
                cs = pool_cs[:, 2 * n:2 * n + 2, :]
                w = WINDOWS[n]
                u = pool_u[:, 2 * n:2 * n + 2, :]
                g.tensor_tensor(sq[:], cs[:, :, PAD:], cs[:, :, PAD - w:PAD - w + S], ALU.subtract).then_inc(s["diff_ready"], 1)
                pool.wait_ge(s["diff_ready"], n + 1)
                g.tensor_tensor(sq[:], sq[:], pool_inv[:, n, :].unsqueeze(1).to_broadcast([P, 2, S]), ALU.mult).then_inc(s["diff_scaled"], 1)
                pool.wait_ge(s["diff_scaled"], n + 1)
                g.tensor_tensor(u, sq[:], u, ALU.subtract).then_inc(s["mixed_ready"], 1)
                pool.wait_ge(s["mixed_ready"], n + 1)

            with pool.Fori(0, 4, 1) as it:
                pool.wait_ge(s["hg_values"], it + 1)
                for t in range(2):
                    last = g.tensor_tensor(hg_bd[:, t], hg_i[:, t, :].unsqueeze(1).to_broadcast([P, 4, CH]),
                                           const("chunk_mask").unsqueeze(2).to_broadcast([P, 4, CH]), ALU.mult)
                last.then_inc(s["hg_bd_ready"], 1)
                pool.wait_ge(s["hg_gsig"], it + 1)
                g.tensor_tensor(tmp[:, 1], tmp[:, 1], hg_sg, ALU.mult).then_inc(s["hg_gg0"], 1)
                pool.wait_ge(s["hg_gg0"], it + 1)
                o, _ = PARAMS["hgrn_g"]
                g.tensor_tensor(tmp[:, 1], tmp[:, 1], par[:, bass.ds(it * 2 + o, 2)].unsqueeze(2).to_broadcast([P, 2, S]),
                                ALU.mult).then_inc(s["hg_gg1"], 1)

            out_stage(C_OUT0, "xa0", 2, 0)
            xq_stage(0)
            out_stage(C_OX0, "mix1", 3, 8, heads=0)
            out_stage(C_OUT1, "xa1", 4, 16)
            xq_stage(XA_HEADS)
            out_stage(C_OX1, "final", 5, 24, final=True, heads=XA_HEADS)


def constants():
    import numpy as np
    p = np.arange(P)[:, None]
    j = np.arange(P)[None, :]
    t = np.arange(S)[None, :]
    parts = {
        "ident": p == j,
        "ones": np.ones((P, P)),
        "neg_tri": -1.0 * (p >= j),
        "neg_ones": -np.ones((P, P)),
        "sb_mask": np.concatenate([p < j, np.ones((P, P)), p < j], 1),
        "hg_mask": (p <= j) & (p // HC == j // HC),
        "reset": np.broadcast_to(t % HC != 0, (P, S)),
        "chunk_mask": p // HC == np.arange(P // HC)[None, :],
    }
    inv = np.stack([1.0 / np.minimum(np.arange(1, S + 1), w) for w in WINDOWS])
    return (np.concatenate([np.asarray(parts[n], np.float32) for n in CONSTS], 1),
            np.ascontiguousarray(np.broadcast_to(inv.astype(np.float32), (P, 4, S))))


def kernel(**inputs):
    import numpy as np
    import concourse.bacc as bacc
    from concourse.bass_utils import run_bass_kernel_spmd

    a = {n: np.ascontiguousarray(v) for n, v in inputs.items()}
    tables, inv_count = constants()

    def columns(v):
        return v.reshape(-1, P).T

    rows = {
        "mix0": a["norm_mix_g"][0], "mix1": a["norm_mix_g"][1], "xa0": a["norm_xa_g"][0], "xa1": a["norm_xa_g"][1],
        "mem0": a["norm_mem_g"][0], "mem1": a["norm_mem_g"][1], "final": a["final_norm_g"],
        "pool_scale": a["pool_scale"][0], "bound0": a["hgrn_lower_bounds"][0], "bound1": a["hgrn_lower_bounds"][1],
        "hgrn_g": a["hgrn_norm_g"][0],
    }
    arrays = {
        "x": a["x"], "mem": a["mem"],
        "params": np.ascontiguousarray(np.concatenate([columns(rows[n]) for n in PARAMS], 1)),
        "consts": tables, "inv_count": inv_count, "pool_w": a["pool_w"],
        "w_in_even": a["w_in_even"], "w_out_even": a["w_out_even"], "w_in_odd": a["w_in_odd"],
        "w_out_odd": a["w_out_odd"], "xa_wq": a["xa_wq"], "xa_wkv": a["xa_wkv"], "xa_wo": a["xa_wo"],
    }
    nc = bacc.Bacc("TRN2", target_bir_lowering=False, num_devices=1)
    handles = [nc.dram_tensor(n, v.shape, F32, kind="ExternalInput").ap() for n, v in arrays.items()]
    out = nc.dram_tensor("out", (1, S, D), F32, kind="ExternalOutput").ap()
    build(nc, *handles, out)
    result = run_bass_kernel_spmd(nc, [arrays], core_ids=[0])
    return result.results[0]["out"]
```

```python
from contextlib import ExitStack

import concourse.bass as bass
from concourse import mybir

ALU = mybir.AluOpType
ACT = mybir.ActivationFunctionType
AX = mybir.AxisListType
F32 = mybir.dt.float32
F32R = mybir.dt.float32r

P = 128
D = 2048
S = 256
KT = D // P
CH = 256
NP = 4
KP = KT // NP
EPS = 1e-6
HC = 32
NHC = S // HC
HEAD = 128
XA_HEADS = 4
XA_SCALE = float(D // XA_HEADS) ** -0.5
SB_SCALE = float(HEAD) ** -0.5
WIDTH = D // 2
BIG = 3.0e38
WINDOWS = (2, 4, 8, 16)
PAD = 16

PARAMS = {}
for _name, _n in (("mix0", 16), ("mix1", 16), ("xa0", 16), ("xa1", 16), ("mem0", 16), ("mem1", 16),
                  ("final", 16), ("pool_scale", 8), ("bound0", 8), ("bound1", 8), ("hgrn_g", 8)):
    PARAMS[_name] = (sum(n for _, n in PARAMS.values()), _n)
N_PARAMS = sum(n for _, n in PARAMS.values())

CONSTS = {}
for _name, _n in (("ident", P), ("ones", P), ("neg_tri", P), ("neg_ones", P), ("sb_mask", 3 * P),
                  ("hg_mask", P), ("reset", S), ("chunk_mask", P // HC)):
    CONSTS[_name] = (sum(n for _, n in CONSTS.values()), _n)
N_CONSTS = sum(n for _, n in CONSTS.values())

C_KV0, C_POOL, C_GATE, C_HGRN, C_OUT0, C_XQ0, C_OX0 = 0, 16, 20, 24, 40, 48, 56
C_KV1, C_SB, C_OUT1, C_XQ1, C_OX1, C_END = 64, 80, 112, 120, 128, 136


def build(nc, x, mem, params, consts, inv_count, pool_w, w_in_even, w_out_even, w_in_odd, w_out_odd,
          xa_wq, xa_wkv, xa_wo, out, stop=None):
    with ExitStack() as ctx:
        def sb(name, shape, dt=F32):
            return ctx.enter_context(nc.sbuf_tensor(name, shape, dt))

        def sem(name):
            return ctx.enter_context(nc.semaphore(name))

        raw = sb("raw", [P, NP, KP, CH])
        wpair = sb("wpair", [P, KT, 2, CH], F32R)
        xpair = sb("xpair", [P, KT, 2, S], F32R)
        ypair = sb("ypair", [P, KT, 2, S], F32R)
        xT = sb("xT", [P, KT, S])
        xkT = sb("xkT", [P, KT, S])
        xv = sb("xv", [P, 2, D])
        par = sb("par", [P, N_PARAMS])
        cst = sb("cst", [P, N_CONSTS])
        rs = sb("rs", [P, S + 2])
        acc = sb("acc", [P, 2, S])
        sq = sb("sq", [P, 2, S])
        tmp = sb("tmp", [P, 2, 2, S])
        mrs = sb("mrs", [P, S + 2])
        small = sb("small", [P, 48])
        SCR = 8192
        scratch = sb("scratch", [P, SCR])
        ps = ctx.enter_context(nc.psum_tensor("ps", [P, 8, 512], F32))

        def prm(name, a=0, n=None):
            o, m = PARAMS[name]
            return par[:, o + a:o + a + (n or m)]

        def const(name):
            o, n = CONSTS[name]
            return cst[:, o:o + n]

        def view(off, *shape):
            n = 1
            for s_ in shape:
                n *= s_
            assert off + n <= SCR
            v = scratch[:, off:off + n]
            if len(shape) == 2:
                v = v.rearrange("p (a b) -> p a b", a=shape[0])
            if len(shape) == 3:
                v = v.rearrange("p (a b c) -> p a b c", a=shape[0], b=shape[1])
            return v

        ident, ones = const("ident"), const("ones")
        rs_row = rs[:, 0:S]
        rs_row2 = rs_row.unsqueeze(1).to_broadcast([P, 2, S])
        rs_col = rs[:, S:S + 2]
        rs_col2 = rs_col.unsqueeze(2).to_broadcast([P, 2, S])
        mrs_row2 = mrs[:, 0:S].unsqueeze(1).to_broadcast([P, 2, S])
        mrs_col2 = mrs[:, S:S + 2].unsqueeze(2).to_broadcast([P, 2, S])
        mem_ss, x_ss = small[:, 0:2], small[:, 2:4]
        diag = sq[:, :, 0:P]
        eps = small[:, 10:11]
        xa_negmax, xa_sum, xa_rsum = small[:, 4:6], small[:, 6:8], small[:, 8:10]
        lb, oml = small[:, 16:24], small[:, 24:32]
        lb_t0, lb_t1 = small[:, 32:40], small[:, 40:48]

        x_nat, junk = view(0, 2, D), view(4096, D)
        pool_u, pool_cs = view(0, 8, S), view(2048, 8, PAD + S)
        pool_inv, pool_wt, pool_sig = view(4224, 4, S), view(5248, 4, 2, S), view(7296, 2, S)
        hg_bd = view(0, 2, 4, CH)
        hg_k, hg_b, hg_sg = view(0, 2, S), view(512, 2, S), view(1024, 2, S)
        hg_ke, hg_eb, hg_kt = view(2048, 2, S), view(2560, 2, S), view(3072, 2, S)
        hg_q, hg_ken, hg_i = view(3584, 2, S), view(4096, 4, P), view(4608, 2, S)
        hg_sc, hg_o, hg_sq = view(4096, 4, P), view(5120, 2, S), view(5632, 2, S)
        hg_st = view(6144, 2, NHC - 1, P)
        out_xg = view(7168, 2, S)
        xq_q, xq_e, xq_pt, xq_v = view(0, 4, S), view(1024, 2, S), view(1536, 2, S), view(2048, 2, 512)
        sb_q, sb_k, sb_v, sb_sg = view(0, 2, S), view(512, 2, S), view(1024, 2, S), view(1536, 2, S)
        sb_l, sb_sp, sb_a = view(2048, 2, 3 * P), view(2816, 2, 3 * P), view(3584, 2, 3 * P)

        ident_in, const_in, x_in, pool_in, out_done = (sem(n) for n in ("ident_in", "const_in", "x_in", "pool_in", "out_done"))
        mem_in = [sem(f"mem_in{p}") for p in range(NP)]
        raw_in = [sem(f"raw_in{p}") for p in range(NP)]
        hi_ready = sem("hi_ready")
        lo_ready = sem("lo_ready")
        piece_done = sem("piece_done")
        evac_done = sem("evac_done")
        xpair_ready = sem("xpair_ready")
        ypair_ready = sem("ypair_ready")
        names = """squares_done diag_ready tr_done tr_hi xt_done eps_ready acc_ready acc_zero stats_done rs_raw rs_root rs_ready mem_keys mem_values
            lb_a lb_b lb_c lb_d lb_ready prod_ready cs_ready diff_ready diff_scaled mixed_ready pool_g pool_sig_ready pool_gs pool_mm pool_y
            y_hi hg_logit hg_sig hg_f0 hg_f1 hg_logf hg_bcum hg_exps hg_d hg_kexp hg_keys hg_ktr hg_kcopy hg_values hg_bd_ready
            hg_u hg_state hg_query hg_scores hg_scores_m hg_omm hg_osq hg_norm hg_r0 hg_r1 hg_gate hg_gsig hg_gg0 hg_gg1 hg_y0 hg_y1
            out_tmp x_new x_sq xg_ready xg_hi
            xa_q xa_vcopy xa_scores xa_max xa_exp xa_rs xa_p xa_ptr xa_pt xa_pv xa_hi
            sb_qr sb_kr sb_z sb_abs sb_exp sb_ln sb_sp0 sb_sp1 sb_cum sb_aexp sb_am sb_vr sb_av sb_gate sb_gsig sb_gg sb_y
            fin_tr fin_out0 fin_out1 cs_zero""".split()
        s = {n: sem(n) for n in names}

        block = ctx.enter_context(nc.Block())

        def wview(w):
            return w.rearrange("(k p) n -> p k n", p=P)

        W_ine, W_oute, W_ino, W_outo = (wview(w[0]) for w in (w_in_even, w_out_even, w_in_odd, w_out_odd))
        W_q, W_kv, W_o = ([wview(w[l]) for l in range(2)] for w in (xa_wq, xa_wkv, xa_wo))

        @block.sync
        def _(sp):
            def load_chunk(c, w, col):
                for p in range(NP):
                    sp.wait_ge(lo_ready, c * 4 + (p + 1))
                    sp.dma_start(raw[:, p], w[:, KP * p:KP * (p + 1), bass.ds(col, CH)]).then_inc(raw_in[p], 16)

            def plain(c0, w, n_chunks, first=0):
                with sp.Fori(first, n_chunks // 2, 1) as it:
                    for j in range(2):
                        load_chunk(it * 2 + (c0 + j), w, it * (2 * CH) + j * CH)

            mem_v = mem[0].rearrange("(r p) d -> p r d", p=P)
            o, n = CONSTS["ident"]
            assert o == 0

            def load_memory(p):
                cols = slice(p * D // NP, (p + 1) * D // NP)
                sp.dma_start(xv[:, :, cols], mem_v[:, :, cols]).then_inc(mem_in[p], 16)

            def load_piece(c, p, w, col):
                sp.wait_ge(lo_ready, c * 4 + (p + 1))
                sp.dma_start(raw[:, p], w[:, KP * p:KP * (p + 1), col:col + CH]).then_inc(raw_in[p], 16)

            sp.dma_start(cst[:, 0:n], consts[:, 0:n]).then_inc(ident_in, 16)
            sp.dma_start(par[:], params).then_inc(ident_in, 16)
            for p in range(NP):
                load_memory(p)
                load_piece(0, p, W_kv[0], 0)
            sp.dma_start(cst[:, n:], consts[:, n:]).then_inc(const_in, 16)
            load_chunk(1, W_kv[0], CH)
            sp.dma_start(x_nat, x[0].rearrange("(r p) d -> p r d", p=P)).then_inc(x_in, 16)
            plain(C_KV0, W_kv[0], 16, first=1)
            sp.wait_ge(s["squares_done"], 4)
            sp.wait_ge(s["tr_done"], 16)
            sp.dma_start(pool_inv, inv_count).then_inc(pool_in, 16)
            sp.dma_start(pool_wt, pool_w[0].rearrange("g (t p) d -> p (g t) d", p=P)).then_inc(pool_in, 16)
            plain(C_POOL, W_ine, 8)
            with sp.Fori(0, 4, 1) as it:
                for j, base in enumerate((3, 4, 2, 5)):
                    load_chunk(it * 4 + (C_HGRN + j), W_ine, it * CH + base * WIDTH)
            plain(C_OUT0, W_oute, 8)
            plain(C_XQ0, W_q[0], 8)
            plain(C_OX0, W_o[0], 8)
            sp.wait_ge(s["xa_pv"], XA_HEADS)
            for p in range(NP):
                load_memory(p)
            plain(C_KV1, W_kv[1], 16)
            with sp.Fori(0, 8, 1) as it:
                for j in range(4):
                    load_chunk(it * 4 + (C_SB + j), W_ino, it * CH + j * D)
            plain(C_OUT1, W_outo, 8)
            plain(C_XQ1, W_q[1], 8)
            plain(C_OX1, W_o[1], 8)
            for r in range(2):
                sp.wait_ge(s[f"fin_out{r}"], 4)
                sp.dma_start(out[0, r * P:(r + 1) * P, :], xv[:, r, :]).then_inc(out_done, 16)
            sp.wait_ge(out_done, 32)

        @block.tensor
        def _(pe):
            mm, tr = nc.tensor.matmul, nc.tensor.transpose

            def piece(c, parity, p, operand, mode, ready=None):
                if p == 0:
                    pe.wait_ge(evac_done, c + 1)
                pe.wait_ge(lo_ready, c * 4 + (p + 5))
                if ready is not None:
                    pe.wait_ge(ready[0], ready[1] + 2 * (p + 1))
                for j in range(2):
                    bank = ps[:, 2 * parity + j, :]
                    for k in range(KP * p, KP * (p + 1)):
                        tile = slice(j * P, (j + 1) * P)
                        still, move = (wpair, operand) if mode == "T" else (operand, wpair)
                        mm(bank, still[:, k, 0, tile], move[:, k].rearrange("p h n -> p (h n)"),
                           start=(k == 0), stop=False)
                        last = mm(bank[:, S:2 * S], still[:, k, 1, tile], move[:, k, 0],
                                  start=False, stop=(k == KT - 1))
                last.then_inc(piece_done, 1)

            def chunk(c, parity, operand, mode, ready=None, hooks=()):
                for p in range(NP):
                    piece(c, parity, p, operand, mode, ready)
                    for at, work in hooks:
                        if at == p:
                            work()

            def transposes(src, batches, landed, free):
                for b in batches:
                    landed(b)
                    if b >= 4:
                        pe.wait_ge(free[0], free[1] + b - 3)
                    for kk in range(2):
                        for r in range(2):
                            k = 2 * b + kk
                            last = tr(ps[:, 4 + b % 4, kk * S + r * P:kk * S + (r + 1) * P],
                                      src[:, r, k * P:(k + 1) * P], ident)
                    last.then_inc(s["tr_done"], 1)

            def spread_sums(n, free):
                pe.wait_ge(s["diag_ready"], n)
                pe.wait_ge(free[0], free[1])
                for r in range(2):
                    last = mm(ps[:, 7, r * P:(r + 1) * P], ones, diag[:, r, :], start=True, stop=True,
                              skip_group_check=True)
                last.then_inc(s["stats_done"], 1)

            def stats(n):
                pe.wait_ge(s["acc_ready"], n)
                bank = ps[:, 7, :]
                for b in range(2):
                    mm(bank[:, 0:S], ones, acc[:, b, :], start=(b == 0), stop=False, skip_group_check=True)
                for r in range(2):
                    for b in range(2):
                        last = mm(bank[:, S + r:S + r + 1], acc[:, b, r * P:(r + 1) * P], ones[:, 0:1],
                                  start=False, stop=(r == 1 and b == 1), skip_group_check=True)
                last.then_inc(s["stats_done"], 1)

            def kv(c0, first=0, ready=None):
                with pe.Fori(first, 4, 1) as it:
                    for j in range(2):
                        chunk(it * 2 + (c0 + j), j, ypair, "T", ready if j == 0 else None)
                with pe.Fori(4, 8, 1) as it:
                    for j in range(2):
                        chunk(it * 2 + (c0 + j), j, ypair, "N")

            def out_stage(c0, ready, heads=None, hooks=()):
                if heads is None:
                    chunk(c0, 0, ypair, "T", ready, hooks)
                else:
                    attend(heads, XA_HEADS - 1, c0, ypair, ready, at=0)
                chunk(c0 + 1, 1, ypair, "T")
                with pe.Fori(1, 4, 1) as it:
                    for j in range(2):
                        chunk(it * 2 + (c0 + j), j, ypair, "T")

            def attend(base, h, c, operand, ready, at):
                n = h + (base + 1)

                def scores():
                    pe.wait_ge(s["xa_q"], n * 2)
                    pe.wait_ge(ypair_ready, h * 2 + (40 if base else 16))
                    for r in range(2):
                        for k in range(4):
                            last = mm(ps[:, 4, r * S:(r + 1) * S], xq_q[:, k, r * P:(r + 1) * P],
                                      xkT[:, bass.ds(h * 4 + k, 1), :].rearrange("p a b -> p (a b)"),
                                      start=(k == 0), stop=(k == 3), skip_group_check=True)
                    last.then_inc(s["xa_scores"], 1)

                def turn():
                    pe.wait_ge(s["xa_p"], n)
                    for m in range(2):
                        for r in range(2):
                            last = tr(ps[:, 5, m * S + r * P:m * S + (r + 1) * P], xq_e[:, r, m * P:(m + 1) * P], ident)
                    last.then_inc(s["xa_ptr"], 1)

                def mix_values():
                    pe.wait_ge(s["xa_pt"], n)
                    pe.wait_ge(s["xa_vcopy"], n)
                    for b in range(4):
                        for m in range(2):
                            last = mm(ps[:, 6 + b // 2, (b % 2) * S:(b % 2 + 1) * S],
                                      xq_v[:, m, b * P:(b + 1) * P], xq_pt[:, m, :],
                                      start=(m == 0), stop=(m == 1), skip_group_check=True)
                    last.then_inc(s["xa_pv"], 1)

                chunk(c, 0, operand, "T", ready, ((at, scores), (at + 1, turn), (at + 2, mix_values)))

            def xq_stage(c0, base, x_ready, n_stats):
                chunk(c0, 0, xpair, "T", x_ready, hooks=((2, lambda: stats(n_stats)),))
                chunk(c0 + 1, 1, xpair, "T")
                with pe.Fori(1, XA_HEADS, 1) as it:
                    attend(base, it - 1, it * 2 + c0, xpair, None, at=1)
                    chunk(it * 2 + (c0 + 1), 1, xpair, "T")

            pe.nop().then_inc(piece_done, 4)
            pe.wait_ge(ident_in, 32)
            transposes(xv, range(8), lambda b: pe.wait_ge(mem_in[b // 2], 16), (ypair_ready, 0))
            pe.wait_ge(const_in, 16)
            chunk(0, 0, ypair, "T", (ypair_ready, 0), ((2, lambda: spread_sums(1, (ypair_ready, 8))),))
            pe.wait_ge(x_in, 16)
            chunk(1, 1, ypair, "T", hooks=((1, lambda: (
                pe.wait_ge(s["rs_raw"], 1),
                transposes(x_nat, range(0, 4), lambda b: None, None))),))
            chunk(2, 0, ypair, "T", hooks=((1, lambda: transposes(x_nat, range(4, 8), lambda b: None, (xpair_ready, 0))),))
            chunk(3, 1, ypair, "T", hooks=((2, lambda: spread_sums(2, (xpair_ready, 8))),))
            kv(C_KV0, first=2)
            for c in range(C_POOL, C_GATE):
                chunk(c, c % 2, xpair, "T")

            def pool_product(g):
                def work():
                    pe.wait_ge(pool_in, 32)
                    pe.wait_ge(s["mixed_ready"], g + 1)
                    if g >= 2:
                        pe.wait_ge(s["pool_y"], 2 * (g - 1))
                    for b in range(2):
                        for t in range(2):
                            last = mm(ps[:, 4 + g % 2, b * S:(b + 1) * S], pool_wt[:, g, t, b * P:(b + 1) * P],
                                      pool_u[:, 2 * g + t, :], start=(t == 0), stop=(t == 1), skip_group_check=True)
                    last.then_inc(s["pool_mm"], 1)
                return work

            for g in range(4):
                chunk(C_GATE + g, g % 2, xpair, "T", hooks=((3, pool_product(g)),))

            def hgrn(it, pipelined):
                def key_transposes():
                    pe.wait_ge(s["hg_keys"], it + 1)
                    for a in range(4):
                        last = tr(ps[:, 4, a * P:(a + 1) * P], hg_ke[:, a // 2, (a % 2) * P:(a % 2 + 1) * P], ident)
                    last.then_inc(s["hg_ktr"], 1)

                def chunk_updates():
                    pe.wait_ge(s["hg_kcopy"], it + 1)
                    pe.wait_ge(s["hg_bd_ready"], it + 1)
                    for a in range(4):
                        h, t = a // 2, a % 2
                        last = mm(ps[:, 4 + a, :], hg_ken[:, a, :], hg_bd[:, t, :, h * P:(h + 1) * P],
                                  start=True, stop=True)
                    last.then_inc(s["hg_u"], 1)

                def intra_scores():
                    pe.wait_ge(s["hg_query"], it + 1)
                    pe.wait_ge(s["hg_state"], it * 14 + 14)
                    for a in range(4):
                        t = slice((a % 2) * P, (a % 2 + 1) * P)
                        last = mm(ps[:, 4, a * P:(a + 1) * P], hg_kt[:, a // 2, t], hg_q[:, a // 2, t],
                                  start=True, stop=True, skip_group_check=True)
                    last.then_inc(s["hg_scores"], 1)

                c = it * 4 + C_HGRN
                chunk(c, 0, xpair, "T", hooks=hgrn_tail(it - 1) if pipelined else ())
                chunk(c + 1, 1, xpair, "N")
                chunk(c + 2, 0, xpair, "T", hooks=((1, key_transposes), (3, chunk_updates)))
                chunk(c + 3, 1, xpair, "T", hooks=((2, intra_scores),))

            def hgrn_tail(it):
                def outputs():
                    pe.wait_ge(s["hg_scores_m"], it + 1)
                    for h in range(2):
                        for t in range(2):
                            mm(ps[:, 5, h * S + t * P:h * S + (t + 1) * P], hg_i[:, t, h * P:(h + 1) * P],
                               hg_sc[:, 2 * h + t, :], start=(h == 0 and t == 0), stop=False, skip_group_check=True)
                        for n in range(1, NHC):
                            last = mm(ps[:, 5, h * S + n * HC:h * S + (n + 1) * HC], hg_st[:, h, n - 1, :],
                                      hg_q[:, h, n * HC:(n + 1) * HC], start=False,
                                      stop=(h == 1 and n == NHC - 1), skip_group_check=True)
                    last.then_inc(s["hg_omm"], 1)

                def head_norm():
                    pe.wait_ge(s["hg_osq"], it + 1)
                    mm(ps[:, 6, :], ones, hg_sq.rearrange("p a b -> p (a b)"),
                       start=True, stop=True).then_inc(s["hg_norm"], 1)

                return ((0, outputs), (1, head_norm))

            hgrn(0, False)
            with pe.Fori(1, 4, 1) as it:
                hgrn(it, True)

            out_stage(C_OUT0, (ypair_ready, 8), hooks=hgrn_tail(3))
            xq_stage(C_XQ0, 0, (xpair_ready, 8), 1)
            out_stage(C_OX0, (ypair_ready, 16), heads=0)
            transposes(xv, range(8), lambda b: pe.wait_ge(mem_in[b // 2], 32), (ypair_ready, 24))
            chunk(C_KV1, 0, ypair, "T", (ypair_ready, 24), hooks=((2, lambda: (
                pe.wait_ge(ypair_ready, 32),
                stats(2))),))
            chunk(C_KV1 + 1, 1, ypair, "T")
            kv(C_KV1, first=1)

            with pe.Fori(0, 8, 1) as it:
                def logits():
                    pe.wait_ge(s["sb_kr"], it + 1)
                    for h in range(2):
                        mm(ps[:, 4 + h, 0:S], sb_k[:, h, 0:P], sb_q[:, h, :],
                           start=True, stop=False, skip_group_check=True)
                        mm(ps[:, 4 + h, S:S + P], sb_k[:, h, P:S], sb_q[:, h, P:S],
                           start=False, stop=False, skip_group_check=True).then_inc(s["sb_z"], 1)

                def cumulate():
                    for h in range(2):
                        pe.wait_ge(s["sb_sp1"], it * 2 + (h + 1))
                        bank = ps[:, 4 + h, :]
                        mm(bank[:, 0:S], const("neg_tri"), sb_sp[:, h, 0:S], start=False, stop=False, skip_group_check=True)
                        mm(bank[:, P:S], const("neg_ones"), sb_sp[:, h, S:S + P], start=False, stop=False, skip_group_check=True)
                        mm(bank[:, S:S + P], const("neg_tri"), sb_sp[:, h, S:S + P], start=False, stop=True,
                           skip_group_check=True).then_inc(s["sb_cum"], 1)

                def mix_values():
                    pe.wait_ge(s["sb_vr"], it + 1)
                    pe.wait_ge(s["sb_am"], it * 2 + 2)
                    for h in range(2):
                        v = slice(h * P, (h + 1) * P)
                        mm(ps[:, 6, h * S:(h + 1) * S], sb_v[:, 0, v], sb_a[:, h, 0:S],
                           start=(h == 0), stop=False, skip_group_check=True)
                        last = mm(ps[:, 6, h * S + P:(h + 1) * S], sb_v[:, 1, v], sb_a[:, h, S:S + P],
                                  start=False, stop=(h == 1), skip_group_check=True)
                    last.then_inc(s["sb_av"], 1)

                c = it * 4 + C_SB
                chunk(c, 0, xpair, "T", (xpair_ready, 16))
                chunk(c + 1, 1, xpair, "T")
                chunk(c + 2, 0, xpair, "N", hooks=((1, logits), (3, cumulate)))
                chunk(c + 3, 1, xpair, "T", hooks=((2, mix_values),))

            out_stage(C_OUT1, (ypair_ready, 32))
            xq_stage(C_XQ1, XA_HEADS, (xpair_ready, 24), 3)
            out_stage(C_OX1, (ypair_ready, 40), heads=XA_HEADS)
            stats(4)
            pe.wait_ge(s["rs_raw"], 6)
            pe.wait_ge(evac_done, C_END + 2)
            for r in range(2):
                for q in range(4):
                    for k in range(4 * q, 4 * q + 4):
                        last = tr(ps[:, 4 * r + q, (k % 4) * P:(k % 4 + 1) * P], xkT[:, k, r * P:(r + 1) * P], ident)
                    last.then_inc(s["fin_tr"], 1)

        @block.scalar
        def _(act):
            fn = nc.scalar.activation

            def split_hi(c, p):
                act.wait_ge(raw_in[p], c * 16 + 16)
                act.wait_ge(piece_done, c * 4 + (p + 1))
                fn(wpair[:, KP * p:KP * (p + 1), 0, :], raw[:, p], ACT.Copy).then_inc(hi_ready, 1)

            def slot(c, steps=(), convert=True):
                for p in range(NP):
                    if convert:
                        split_hi(c + 1, p)
                    for at, work in steps:
                        if at == p:
                            work()

            def rs_root(n, dst=rs):
                act.wait_ge(s["rs_raw"], n)
                fn(dst[:, :], dst[:, :], ACT.Sqrt).then_inc(s["rs_root"], 1)

            def squares(n, src, sums):
                for r in range(2):
                    if n + r:
                        act.wait_ge(s["squares_done"], n + r)
                    fn(junk, src[:, r, :], ACT.Square, accum_out=sums[:, r:r + 1]).then_inc(s["squares_done"], 1)

            def transposed_x(batches):
                for b in batches:
                    act.wait_ge(s["tr_done"], 8 + b + 1)
                    fn(xT[:, 2 * b:2 * b + 2, :], ps[:, 4 + b % 4, :].rearrange("p (a b) -> p a b", a=2), ACT.Copy)
                    for kk in range(2):
                        last = fn(xpair[:, 2 * b + kk, 0, :], ps[:, 4 + b % 4, kk * S:(kk + 1) * S], ACT.Copy,
                                  scale=prm("mix0", 2 * b + kk, 1))
                    last.then_inc(s["tr_hi"], 1)

            def transposed_mem(gain, tr0):
                for b in range(8):
                    act.wait_ge(s["tr_done"], tr0 + b + 1)
                    for kk in range(2):
                        last = fn(ypair[:, 2 * b + kk, 0, :], ps[:, 4 + b % 4, kk * S:(kk + 1) * S], ACT.Copy,
                                  scale=prm(gain, 2 * b + kk, 1))
                    last.then_inc(s["tr_hi"], 1)

            def out_stage(c0, heads=None, pair=True, steps=()):
                def hi(it, j):
                    def work():
                        act.wait_ge(s["xg_ready"], n_xg + it * 2 + (j + 1))
                        k = it * 4 + 2 * j
                        fn(xpair[:, bass.ds(k, 2), 0, :], out_xg, ACT.Copy).then_inc(s["xg_hi"], 1)
                    return work
                n_xg = xg_count[0]
                xg_count[0] += 8
                if heads is not None:
                    steps = attend(heads, XA_HEADS - 1, at=0)
                slot(c0, steps + (((3, hi(0, 0)),) if pair else ()))
                slot(c0 + 1, ((3, hi(0, 1)),) if pair else ())
                last_it = 3 if c0 == C_OX1 else 4
                with act.Fori(1, last_it, 1) as it:
                    for j in range(2):
                        slot(it * 2 + (c0 + j), ((3, hi(it, j)),) if pair else ())
                if c0 == C_OX1:
                    slot(C_END - 2)
                    slot(C_END - 1, convert=False)

            xg_count = [0]

            def attend(base, h, at):
                n = h + (base + 1)

                def exps():
                    act.wait_ge(s["xa_max"], n)
                    for r in range(2):
                        last = fn(xq_e[:, r, :], ps[:, 4, r * S:(r + 1) * S], ACT.Exp,
                                  bias=xa_negmax[:, r:r + 1], accum_out=xa_sum[:, r:r + 1])
                    last.then_inc(s["xa_exp"], 1)

                def copy_pt():
                    act.wait_ge(s["xa_ptr"], n)
                    fn(xq_pt.rearrange("p a b -> p (a b)"), ps[:, 5, :], ACT.Copy).then_inc(s["xa_pt"], 1)

                def hi():
                    act.wait_ge(s["xa_pv"], n)
                    for b in range(2):
                        fn(ypair[:, bass.ds(h * 4 + 2 * b, 2), 0, :],
                           ps[:, 6 + b, :].rearrange("p (a b) -> p a b", a=2), ACT.Copy).then_inc(s["xa_hi"], 1)
                return ((at, exps), (at + 1, copy_pt), (at + 2, hi))

            def xq_stage(c0, base, n_stats):
                slot(c0, ((3, lambda: rs_root(n_stats)),))
                slot(c0 + 1)
                with act.Fori(1, XA_HEADS, 1) as it:
                    slot(it * 2 + c0, attend(base, it - 1, at=1))
                    slot(it * 2 + (c0 + 1))

            act.wait_ge(s["eps_ready"], 1)
            act.wait_ge(ident_in, 32)
            split_hi(0, 0)
            transposed_mem("mem0", 0)
            for p in range(1, NP):
                split_hi(0, p)
            squares(0, xv, mem_ss)
            slot(0, ((3, lambda: rs_root(1, mrs)),))

            def bounds():
                act.wait_ge(s["lb_a"], 2)
                fn(lb_t0, lb_t0, ACT.Exp)
                fn(lb_t1, lb_t1, ACT.Exp).then_inc(s["lb_b"], 1)

            slot(1, ((2, lambda: transposed_x(range(0, 4))),))
            slot(2, ((2, lambda: transposed_x(range(4, 8))),))
            slot(3, ((0, lambda: squares(2, x_nat, x_ss)), (3, lambda: rs_root(2))))
            with act.Fori(2, C_POOL // 2, 1) as it:
                for j in range(2):
                    slot(it * 2 + j)
            bounds()
            for c in range(C_POOL, C_GATE):
                slot(c)
            for g in range(4):
                def gate_sigmoid():
                    act.wait_ge(s["pool_g"], g + 1)
                    fn(pool_sig, tmp[:, g % 2], ACT.Sigmoid).then_inc(s["pool_sig_ready"], 1)
                    act.wait_ge(s["pool_y"], 2 * (g + 1))
                    fn(ypair[:, 2 * g:2 * g + 2, 0, :], tmp[:, g % 2], ACT.Copy).then_inc(s["y_hi"], 1)
                slot(C_GATE + g, ((3, gate_sigmoid),))

            def hgrn(it, pipelined):
                def sigmoid():
                    act.wait_ge(s["hg_logit"], it + 1)
                    fn(hg_k, hg_k, ACT.Sigmoid).then_inc(s["hg_sig"], 1)

                def log_f():
                    nc.scalar.preload_act_table_set("natural_log_exp_and_others")
                    act.wait_ge(s["hg_f1"], it + 1)
                    fn(hg_ke, hg_k, ACT.Ln).then_inc(s["hg_logf"], 1)

                def exps():
                    act.wait_ge(s["hg_bcum"], it + 1)
                    fn(hg_eb, hg_b, ACT.Exp)
                    fn(hg_kt, hg_b, ACT.Exp, scale=-1.0).then_inc(s["hg_exps"], 1)

                def key_exp():
                    act.wait_ge(s["hg_d"], it + 1)
                    fn(hg_ke, hg_ke, ACT.Exp).then_inc(s["hg_kexp"], 1)

                def key_copy():
                    act.wait_ge(s["hg_ktr"], it + 1)
                    fn(hg_ken.rearrange("p a b -> p (a b)"), ps[:, 4, :], ACT.Copy).then_inc(s["hg_kcopy"], 1)

                def gate():
                    act.wait_ge(s["hg_gate"], it + 1)
                    fn(hg_sg, tmp[:, 1], ACT.Sigmoid).then_inc(s["hg_gsig"], 1)

                c = it * 4 + C_HGRN
                slot(c, (hgrn_tail(it - 1) if pipelined else ()) + ((3, sigmoid),))
                slot(c + 1, ((0, log_f), (1, exps), (2, key_exp)))
                slot(c + 2, ((2, key_copy),))
                slot(c + 3, ((3, gate),))

            def hgrn_tail(it):
                def output_squares():
                    nc.scalar.preload_act_table_set("natural_log_exp_and_others")
                    act.wait_ge(s["hg_omm"], it + 1)
                    o = ps[:, 5, :].rearrange("p (a b) -> p a b", a=2)
                    fn(hg_sq, o, ACT.Square)
                    fn(hg_o, o, ACT.Copy).then_inc(s["hg_osq"], 1)

                def norm_factor():
                    act.wait_ge(s["hg_norm"], it + 1)
                    fn(hg_ke, ps[:, 6, :].rearrange("p (a b) -> p a b", a=2), ACT.Ln, scale=1.0 / HEAD,
                       bias=eps).then_inc(s["hg_r0"], 1)
                    act.wait_ge(s["hg_r0"], it + 1)
                    fn(hg_ke, hg_ke, ACT.Exp, scale=-0.5).then_inc(s["hg_r1"], 1)
                    act.wait_ge(s["hg_y1"], it + 1)
                    fn(ypair[:, bass.ds(it * 2 + 8, 2), 0, :], hg_o, ACT.Copy).then_inc(s["y_hi"], 1)
                return ((0, output_squares), (1, norm_factor))

            hgrn(0, False)
            with act.Fori(1, 4, 1) as it:
                hgrn(it, True)

            out_stage(C_OUT0, steps=hgrn_tail(3))
            xq_stage(C_XQ0, 0, 3)
            out_stage(C_OX0, heads=0)
            transposed_mem("mem1", 16)
            slot(C_KV1, ((3, lambda: rs_root(4)),))
            slot(C_KV1 + 1)
            with act.Fori(1, 8, 1) as it:
                for j in range(2):
                    slot(it * 2 + (C_KV1 + j))

            with act.Fori(0, 8, 1) as it:
                def softplus():
                    nc.scalar.preload_act_table_set("natural_log_exp_and_others")
                    for h in range(2):
                        act.wait_ge(s["sb_z"], it * 2 + (h + 1))
                        fn(sb_l[:, h, :], ps[:, 4 + h, 0:3 * P], ACT.Abs).then_inc(s["sb_abs"], 1)
                    for h in range(2):
                        act.wait_ge(s["sb_abs"], it * 2 + (h + 1))
                        fn(sb_l[:, h, :], sb_l[:, h, :], ACT.Exp, scale=-1.0).then_inc(s["sb_exp"], 1)
                    for h in range(2):
                        act.wait_ge(s["sb_exp"], it * 2 + (h + 1))
                        fn(sb_l[:, h, :], sb_l[:, h, :], ACT.Ln, bias=1.0).then_inc(s["sb_ln"], 1)

                def weights():
                    for h in range(2):
                        act.wait_ge(s["sb_cum"], it * 2 + (h + 1))
                        fn(sb_a[:, h, :], ps[:, 4 + h, 0:3 * P], ACT.Exp).then_inc(s["sb_aexp"], 1)

                def gate():
                    act.wait_ge(s["sb_gate"], it + 1)
                    fn(sb_sg, tmp[:, 1], ACT.Sigmoid).then_inc(s["sb_gsig"], 1)
                    act.wait_ge(s["sb_y"], it + 1)
                    fn(ypair[:, bass.ds(it * 2, 2), 0, :], tmp[:, 1], ACT.Copy).then_inc(s["y_hi"], 1)

                c = it * 4 + C_SB
                slot(c)
                slot(c + 1)
                slot(c + 2, ((2, softplus),))
                slot(c + 3, ((0, weights), (3, gate)))

            out_stage(C_OUT1)
            xq_stage(C_XQ1, XA_HEADS, 5)
            out_stage(C_OX1, heads=XA_HEADS, pair=False)
            rs_root(6)
            act.wait_ge(s["rs_ready"], 6)
            for n in range(0, 8, 2):
                act.wait_ge(s["fin_tr"], n + 1)
                fn(xv[:, n // 4, (n % 4) * 512:(n % 4 + 1) * 512], ps[:, n, :], ACT.Copy,
                   scale=rs[:, S + n // 4:S + n // 4 + 1]).then_inc(s[f"fin_out{n // 4}"], 1)

        @block.vector
        def _(dve):
            v = nc.vector

            def split_lo(c, p):
                dve.wait_ge(hi_ready, c * 4 + (p + 1))
                kp = slice(KP * p, KP * (p + 1))
                v.tensor_tensor(wpair[:, kp, 1, :], raw[:, p], wpair[:, kp, 0, :].bitcast(F32),
                                ALU.subtract).then_inc(lo_ready, 1)

            def slot(c, steps=(), convert=True):
                for p in range(NP):
                    if convert:
                        split_lo(c + 1, p)
                    for at, work in steps:
                        if at == p:
                            work()

            def take(c, parity, dst):
                dve.wait_ge(piece_done, c * 4 + 8)
                v.tensor_reduce(dst, ps[:, 2 * parity:2 * parity + 2, :].rearrange("p j (h n) -> p j n h", h=2),
                                AX.X, ALU.add).then_inc(evac_done, 1)
                dve.wait_ge(evac_done, c + 3)

            def rs_step(n, dst=rs, sums=None):
                dve.wait_ge(s["stats_done"], n)
                width = S if sums is not None else S + 2
                if sums is not None:
                    v.tensor_scalar(dst[:, S:S + 2], sums, 1.0 / D, EPS, ALU.mult, ALU.add)
                v.tensor_scalar(dst[:, 0:width], ps[:, 7, 0:width], 1.0 / D, EPS, ALU.mult, ALU.add).then_inc(s["rs_raw"], 1)
                dve.wait_ge(s["rs_root"], n)
                v.reciprocal(dst[:, :], dst[:, :]).then_inc(s["rs_ready"], 1)
                dve.wait_ge(s["rs_ready"], n)

            def diagonal(n, sums):
                dve.wait_ge(s["squares_done"], 2 * n)
                if n > 1:
                    dve.wait_ge(s["stats_done"], n - 1)
                for r in range(2):
                    last = v.tensor_scalar(diag[:, r, :], ident, sums[:, r:r + 1], None, ALU.mult)
                last.then_inc(s["diag_ready"], 1)

            def transposed_lo(dst, gain, hi0, done, batches=range(8)):
                for b in batches:
                    dve.wait_ge(s["tr_hi"], hi0 + b + 1)
                    for kk in range(2):
                        k = 2 * b + kk
                        last = v.scalar_tensor_tensor(dst[:, k, 1, :], ps[:, 4 + b % 4, kk * S:(kk + 1) * S],
                                                      prm(gain, k, 1), dst[:, k, 0, :].bitcast(F32),
                                                      ALU.mult, ALU.subtract)
                    last.then_inc(done, 1)

            def keys(c0, it, j):
                def work():
                    take(it * 2 + (c0 + j), j, tmp[:, j])
                    v.tensor_tensor(xkT[:, bass.ds(it * 4 + 2 * j, 2), :], tmp[:, j], mrs_row2, ALU.mult).then_inc(s["mem_keys"], 1)
                return work

            def kv(c0, first):
                with dve.Fori(first, 4, 1) as it:
                    for j in range(2):
                        slot(it * 2 + (c0 + j), ((3, keys(c0, it, j)),))
                with dve.Fori(0, 4, 1) as it:
                    for j in range(2):
                        def values():
                            take(it * 2 + (c0 + 8 + j), j, tmp[:, j])
                            v.tensor_tensor(xv[:, :, bass.ds(it * (2 * CH) + j * CH, CH)], tmp[:, j], mrs_col2,
                                            ALU.mult).then_inc(s["mem_values"], 1)
                        slot(it * 2 + (c0 + 8 + j), ((3, values),))

            def attend(base, h, at):
                n = h + (base + 1)

                def softmax():
                    dve.wait_ge(s["xa_scores"], n)
                    v.tensor_reduce(xa_negmax, ps[:, 4, :].rearrange("p (a b) -> p a b", a=2), AX.X, ALU.max,
                                    negate=True).then_inc(s["xa_max"], 1)
                    dve.wait_ge(s["xa_exp"], n)
                    v.reciprocal(xa_rsum, xa_sum).then_inc(s["xa_rs"], 1)
                    dve.wait_ge(s["xa_rs"], n)
                    for r in range(2):
                        last = v.tensor_scalar(xq_e[:, r, :], xq_e[:, r, :], xa_rsum[:, r:r + 1], None, ALU.mult)
                    last.then_inc(s["xa_p"], 1)

                def lo():
                    for b in range(2):
                        dve.wait_ge(s["xa_hi"], n * 2 + (b - 1))
                        v.tensor_tensor(ypair[:, bass.ds(h * 4 + 2 * b, 2), 1, :],
                                        ps[:, 6 + b, :].rearrange("p (a b) -> p a b", a=2),
                                        ypair[:, bass.ds(h * 4 + 2 * b, 2), 0, :].bitcast(F32),
                                        ALU.subtract).then_inc(ypair_ready, 1)
                return ((at, softmax), (at + 2, lo))

            def xq_stage(c0, base, n_stats):
                def query(it, j):
                    def work():
                        take(it * 2 + (c0 + j), j, tmp[:, j])
                        v.scalar_tensor_tensor(xq_q[:, 2 * j:2 * j + 2, :], tmp[:, j], XA_SCALE, rs_row2,
                                               ALU.mult, ALU.mult).then_inc(s["xa_q"], 1)
                    return work
                slot(c0, ((3, lambda: rs_step(n_stats)), (3, query(0, 0))))
                slot(c0 + 1, ((3, query(0, 1)),))
                with dve.Fori(1, XA_HEADS, 1) as it:
                    slot(it * 2 + c0, attend(base, it - 1, at=1) + ((3, query(it, 0)),))
                    slot(it * 2 + (c0 + 1), ((3, query(it, 1)),))

            out_count = [0]

            def out_stage(c0, heads=None, pair=True, steps=()):
                n0 = out_count[0]
                out_count[0] += 8

                def residual(it, j):
                    def work():
                        if not pair:
                            dve.wait_ge(s["x_new"], n0 + it * 2 + (j - 1))
                        take(it * 2 + (c0 + j), j, tmp[:, j])
                        v.nop().then_inc(s["out_tmp"], 1)
                        if pair:
                            dve.wait_ge(s["xg_hi"], n0 + it * 2 + (j + 1))
                            v.tensor_tensor(xpair[:, bass.ds(it * 4 + 2 * j, 2), 1, :], out_xg,
                                            xpair[:, bass.ds(it * 4 + 2 * j, 2), 0, :].bitcast(F32),
                                            ALU.subtract).then_inc(xpair_ready, 1)
                    return work
                if heads is not None:
                    steps = attend(heads, XA_HEADS - 1, at=0)
                slot(c0, steps + ((3, residual(0, 0)),))
                slot(c0 + 1, ((3, residual(0, 1)),))
                last_it = 3 if c0 == C_OX1 else 4
                with dve.Fori(1, last_it, 1) as it:
                    for j in range(2):
                        slot(it * 2 + (c0 + j), ((3, residual(it, j)),))
                if c0 == C_OX1:
                    slot(C_END - 2, ((3, residual(3, 0)),))
                    slot(C_END - 1, ((3, residual(3, 1)),), convert=False)

            v.memset(eps, EPS).then_inc(s["eps_ready"], 1)
            v.nop().then_inc(lo_ready, 4)
            v.nop().then_inc(evac_done, 2)
            dve.wait_ge(ident_in, 32)
            split_lo(0, 0)
            transposed_lo(ypair, "mem0", 0, ypair_ready)
            for p in range(1, NP):
                split_lo(0, p)
            diagonal(1, mem_ss)
            slot(0, ((3, lambda: rs_step(1, mrs, mem_ss)), (3, keys(0, 0, 0))))
            slot(1, ((2, lambda: transposed_lo(xpair, "mix0", 8, xpair_ready, range(0, 4))), (3, keys(0, 0, 1))))
            slot(2, ((2, lambda: transposed_lo(xpair, "mix0", 8, xpair_ready, range(4, 8))), (3, keys(0, 1, 0))))
            slot(3, ((1, lambda: diagonal(2, x_ss)), (3, lambda: rs_step(2, rs, x_ss)), (3, keys(0, 1, 1))))
            v.tensor_tensor(lb, prm("bound0"), prm("bound1"), ALU.max).then_inc(s["lb_a"], 1)
            dve.wait_ge(s["lb_a"], 1)
            v.tensor_tensor(lb_t0, prm("bound0"), lb, ALU.subtract)
            v.tensor_tensor(lb_t1, prm("bound1"), lb, ALU.subtract).then_inc(s["lb_a"], 1)
            kv(C_KV0, first=2)
            dve.wait_ge(s["lb_b"], 1)
            v.tensor_tensor(lb_t1, lb_t0, lb_t1, ALU.add).then_inc(s["lb_c"], 1)
            dve.wait_ge(s["lb_c"], 1)
            v.reciprocal(lb_t1, lb_t1).then_inc(s["lb_c"], 1)
            dve.wait_ge(s["lb_c"], 2)
            v.tensor_tensor(lb, lb_t0, lb_t1, ALU.mult).then_inc(s["lb_d"], 1)
            dve.wait_ge(s["lb_d"], 1)
            v.tensor_scalar(oml, lb, -1.0, 1.0, ALU.mult, ALU.add).then_inc(s["lb_ready"], 1)

            for c in range(C_POOL, C_GATE):
                def pool_input():
                    b = 2 * (c - C_POOL)
                    take(c, c % 2, tmp[:, c % 2])
                    v.tensor_tensor(pool_u[:, b:b + 2, :], tmp[:, c % 2], rs_row2, ALU.mult).then_inc(s["prod_ready"], 1)
                    dve.wait_ge(s["prod_ready"], c - C_POOL + 1)
                    if c == C_POOL:
                        dve.wait_ge(s["cs_zero"], 1)
                    for k in range(b, b + 2):
                        last = v.tensor_tensor_scan(pool_cs[:, k, PAD:], ones[:, 0:1].to_broadcast([P, S]),
                                                    pool_u[:, k, :], 0.0, ALU.mult, ALU.add)
                    last.then_inc(s["cs_ready"], 1)
                slot(c, ((3, pool_input),))
            for g in range(4):
                def pool_gate():
                    t = tmp[:, g % 2]
                    take(C_GATE + g, g % 2, t)
                    v.tensor_tensor(t, t, rs_row2, ALU.mult).then_inc(s["pool_g"], 1)
                    dve.wait_ge(s["pool_sig_ready"], g + 1)
                    v.tensor_tensor(t, t, pool_sig, ALU.mult).then_inc(s["pool_gs"], 1)
                    dve.wait_ge(s["pool_gs"], g + 1)
                    dve.wait_ge(s["pool_mm"], g + 1)
                    for b in range(2):
                        v.scalar_tensor_tensor(t[:, b, :], ps[:, 4 + g % 2, b * S:(b + 1) * S],
                                               prm("pool_scale", 2 * g + b, 1), t[:, b, :],
                                               ALU.mult, ALU.mult).then_inc(s["pool_y"], 1)
                    dve.wait_ge(s["y_hi"], g + 1)
                    v.tensor_tensor(ypair[:, 2 * g:2 * g + 2, 1, :], t, ypair[:, 2 * g:2 * g + 2, 0, :].bitcast(F32),
                                    ALU.subtract).then_inc(ypair_ready, 1)
                slot(C_GATE + g, ((3, pool_gate),))

            def hgrn(it, pipelined):
                c = it * 4 + C_HGRN

                def bc(ap):
                    return ap.unsqueeze(2).to_broadcast([P, 2, S])

                def logits():
                    take(c, 0, tmp[:, 0])
                    v.tensor_tensor(hg_k, tmp[:, 0], rs_row2, ALU.mult).then_inc(s["hg_logit"], 1)

                def forget():
                    dve.wait_ge(s["hg_sig"], it + 1)
                    v.tensor_tensor(hg_k, hg_k, bc(oml[:, bass.ds(it * 2, 2)]), ALU.mult).then_inc(s["hg_f0"], 1)
                    dve.wait_ge(s["hg_f0"], it + 1)
                    v.tensor_tensor(hg_k, hg_k, bc(lb[:, bass.ds(it * 2, 2)]), ALU.add).then_inc(s["hg_f1"], 1)

                def cumulate():
                    dve.wait_ge(s["hg_logf"], it + 1)
                    for h in range(2):
                        last = v.tensor_tensor_scan(hg_b[:, h, :], const("reset"), hg_ke[:, h, :], 0.0, ALU.mult, ALU.add)
                    last.then_inc(s["hg_bcum"], 1)
                    v.tensor_scalar(hg_k, hg_k, -1.0, 1.0, ALU.mult, ALU.add)

                def key_exponent():
                    b4 = hg_b.rearrange("p a (n c) -> p (a n) c", c=HC)
                    dve.wait_ge(s["hg_bcum"], it + 1)
                    v.tensor_tensor(hg_ke.rearrange("p a (n c) -> p (a n) c", c=HC),
                                    b4[:, :, HC - 1:HC].to_broadcast([P, 2 * NHC, HC]), b4,
                                    ALU.subtract).then_inc(s["hg_d"], 1)

                def keys():
                    dve.wait_ge(s["hg_kexp"], it + 1)
                    dve.wait_ge(s["hg_exps"], it + 1)
                    v.tensor_tensor(hg_kt, hg_kt, hg_k, ALU.mult)
                    v.tensor_tensor(hg_ke, hg_ke, hg_k, ALU.mult).then_inc(s["hg_keys"], 1)

                def values():
                    take(c + 1, 1, tmp[:, 1])
                    v.tensor_tensor(hg_i, tmp[:, 1], rs_col2, ALU.mult).then_inc(s["hg_values"], 1)

                def states():
                    dve.wait_ge(s["hg_u"], it + 1)
                    for n in range(NHC - 1):
                        for h in range(2):
                            u = ps[:, 4 + 2 * h + n // 4, (n % 4) * P:(n % 4 + 1) * P]
                            if n == 0:
                                v.tensor_copy(hg_st[:, h, 0, :], u).then_inc(s["hg_state"], 1)
                                continue
                            at = n * HC + HC - 1
                            dve.wait_ge(s["hg_state"], it * 14 + (2 * (n - 1) + h + 1))
                            v.scalar_tensor_tensor(hg_st[:, h, n, :], hg_st[:, h, n - 1, :], hg_eb[:, h, at:at + 1], u,
                                                   ALU.mult, ALU.add).then_inc(s["hg_state"], 1)

                def queries():
                    take(c + 2, 0, tmp[:, 0])
                    v.tensor_tensor(hg_q, tmp[:, 0], rs_row2, ALU.mult).then_inc(s["prod_ready"], 1)
                    dve.wait_ge(s["prod_ready"], it + 5)
                    v.tensor_tensor(hg_q, hg_q, hg_eb, ALU.mult).then_inc(s["hg_query"], 1)

                def mask_scores():
                    dve.wait_ge(s["hg_scores"], it + 1)
                    v.tensor_tensor(hg_sc, ps[:, 4, :].rearrange("p (a b) -> p a b", a=4),
                                    const("hg_mask").unsqueeze(1).to_broadcast([P, 4, P]), ALU.mult).then_inc(s["hg_scores_m"], 1)

                def gate():
                    take(c + 3, 1, tmp[:, 1])
                    v.tensor_tensor(tmp[:, 1], tmp[:, 1], rs_row2, ALU.mult).then_inc(s["hg_gate"], 1)

                slot(c, (hgrn_tail(it - 1) if pipelined else ()) + ((3, logits),))
                slot(c + 1, ((0, forget), (1, cumulate), (2, key_exponent), (3, keys), (3, values)))
                slot(c + 2, ((3, queries),))
                slot(c + 3, ((0, states), (2, mask_scores), (3, gate)))

            def hgrn_tail(it):
                def finish():
                    dve.wait_ge(s["hg_r1"], it + 1)
                    v.tensor_tensor(hg_o, hg_o, hg_ke, ALU.mult).then_inc(s["hg_y0"], 1)
                    dve.wait_ge(s["hg_y0"], it + 1)
                    dve.wait_ge(s["hg_gg1"], it + 1)
                    v.tensor_tensor(hg_o, hg_o, tmp[:, 1], ALU.mult).then_inc(s["hg_y1"], 1)
                    dve.wait_ge(s["y_hi"], it + 5)
                    v.tensor_tensor(ypair[:, bass.ds(it * 2 + 8, 2), 1, :], hg_o,
                                    ypair[:, bass.ds(it * 2 + 8, 2), 0, :].bitcast(F32), ALU.subtract).then_inc(ypair_ready, 1)
                return ((1, finish),)

            hgrn(0, False)
            with dve.Fori(1, 4, 1) as it:
                hgrn(it, True)

            out_stage(C_OUT0, steps=hgrn_tail(3))
            xq_stage(C_XQ0, 0, 3)
            out_stage(C_OX0, heads=0)
            transposed_lo(ypair, "mem1", 16, ypair_ready)
            slot(C_KV1, ((3, lambda: rs_step(4)), (3, keys(C_KV1, 0, 0))))
            slot(C_KV1 + 1, ((3, keys(C_KV1, 0, 1)),))
            kv(C_KV1, first=1)

            with dve.Fori(0, 8, 1) as it:
                c = it * 4 + C_SB

                def queries():
                    take(c, 0, tmp[:, 0])
                    v.scalar_tensor_tensor(sb_q, tmp[:, 0], SB_SCALE, rs_row2, ALU.mult, ALU.mult).then_inc(s["sb_qr"], 1)

                def keys():
                    take(c + 1, 1, tmp[:, 1])
                    v.tensor_tensor(sb_k, tmp[:, 1], rs_row2, ALU.mult).then_inc(s["sb_kr"], 1)

                def softplus():
                    for h in range(2):
                        dve.wait_ge(s["sb_ln"], it * 2 + (h + 1))
                        v.scalar_tensor_tensor(sb_sp[:, h, :], ps[:, 4 + h, 0:3 * P], 0.0, sb_l[:, h, :],
                                               ALU.max, ALU.add).then_inc(s["sb_sp0"], 1)
                    for h in range(2):
                        dve.wait_ge(s["sb_sp0"], it * 2 + (h + 1))
                        v.tensor_tensor(sb_sp[:, h, :], sb_sp[:, h, :], const("sb_mask"), ALU.mult).then_inc(s["sb_sp1"], 1)

                def weights():
                    for h in range(2):
                        dve.wait_ge(s["sb_aexp"], it * 2 + (h + 1))
                        v.scalar_tensor_tensor(sb_a[:, h, :], sb_a[:, h, :], BIG, const("sb_mask"),
                                               ALU.min, ALU.mult).then_inc(s["sb_am"], 1)

                def values():
                    take(c + 2, 0, tmp[:, 0])
                    v.tensor_tensor(sb_v, tmp[:, 0], rs_col2, ALU.mult).then_inc(s["sb_vr"], 1)

                def gate():
                    t = tmp[:, 1]
                    take(c + 3, 1, t)
                    v.tensor_tensor(t, t, rs_row2, ALU.mult).then_inc(s["sb_gate"], 1)
                    dve.wait_ge(s["sb_gsig"], it + 1)
                    v.tensor_tensor(t, t, sb_sg, ALU.mult).then_inc(s["sb_gg"], 1)
                    dve.wait_ge(s["sb_gg"], it + 1)
                    dve.wait_ge(s["sb_av"], it + 1)
                    v.tensor_tensor(t, ps[:, 6, :].rearrange("p (a b) -> p a b", a=2), t, ALU.mult).then_inc(s["sb_y"], 1)
                    dve.wait_ge(s["y_hi"], it + 9)
                    v.tensor_tensor(ypair[:, bass.ds(it * 2, 2), 1, :], t,
                                    ypair[:, bass.ds(it * 2, 2), 0, :].bitcast(F32), ALU.subtract).then_inc(ypair_ready, 1)

                slot(c, ((3, queries),))
                slot(c + 1, ((3, keys),))
                slot(c + 2, ((2, softplus), (3, values)))
                slot(c + 3, ((0, weights), (3, gate)))

            out_stage(C_OUT1)
            xq_stage(C_XQ1, XA_HEADS, 5)
            out_stage(C_OX1, heads=XA_HEADS, pair=False)
            rs_step(6)
            for n in range(1, 8, 2):
                dve.wait_ge(s["fin_tr"], n + 1)
                v.tensor_scalar(xv[:, n // 4, (n % 4) * 512:(n % 4 + 1) * 512], ps[:, n, :],
                                rs[:, S + n // 4:S + n // 4 + 1], None, ALU.mult).then_inc(s[f"fin_out{n // 4}"], 1)

        @block.gpsimd
        def _(pool):
            g = nc.gpsimd
            sq_count = [0]

            def zero_acc(n):
                if n:
                    pool.wait_ge(s["stats_done"], n + 2)
                g.memset(acc[:], 0.0).then_inc(s["acc_zero"], 1)
                pool.wait_ge(s["acc_zero"], n + 1)

            def add_squares(block_ap, it, n0, last=False):
                g.tensor_tensor(sq[:], block_ap, block_ap, ALU.mult).then_inc(s["x_sq"], 1)
                pool.wait_ge(s["x_sq"], it + (n0 + 1))
                ins = g.tensor_tensor(acc[:], acc[:], sq[:], ALU.add)
                return ins

            def out_stage(c0, gain, n_stats, n0, final=False, heads=None):
                zero_acc(n_stats)

                def residual(it, j):
                    i = it * 2 + j
                    blk = bass.ds(it * 4 + 2 * j, 2)
                    pool.wait_ge(s["out_tmp"], i + (n0 + 1))
                    g.tensor_tensor(xT[:, blk, :], xT[:, blk, :], tmp[:, j], ALU.add).then_inc(s["x_new"], 1)
                    pool.wait_ge(s["x_new"], i + (n0 + 1))
                    o, _ = PARAMS[gain]
                    gb = par[:, bass.ds(it * 4 + (2 * j + o), 2)].unsqueeze(2).to_broadcast([P, 2, S])
                    dst = xkT[:, blk, :] if final else out_xg
                    g.tensor_tensor(dst, xT[:, blk, :], gb, ALU.mult).then_inc(s["xg_ready"], 1)
                    add_squares(xT[:, blk, :], i, n0).then_inc(s["xt_done"], 1)
                    pool.wait_ge(s["xt_done"], i + (n0 + 1))

                if heads is not None:
                    residual(0, 0)
                    residual(0, 1)
                with pool.Fori(0 if heads is None else 1, 4, 1) as it:
                    for j in range(2):
                        residual(it, j)
                pool.nop().then_inc(s["acc_ready"], 1)

            def copy_values(base, h):
                n = h + (base + 1)
                g.tensor_copy(xq_v, xv[:, :, bass.ds(h * 512, 512)]).then_inc(s["xa_vcopy"], 1)

            def xq_stage(base):
                copy_values(base, 0)
                with pool.Fori(1, XA_HEADS, 1) as it:
                    pool.wait_ge(s["xa_pv"], it + base)
                    copy_values(base, it)

            pool.wait_ge(s["squares_done"], 4)
            pool.wait_ge(s["tr_done"], 16)
            g.memset(pool_cs[:, :, 0:PAD], 0.0).then_inc(s["cs_zero"], 1)
            pool.wait_ge(pool_in, 32)
            for n in range(4):
                pool.wait_ge(s["cs_ready"], n + 1)
                cs = pool_cs[:, 2 * n:2 * n + 2, :]
                w = WINDOWS[n]
                u = pool_u[:, 2 * n:2 * n + 2, :]
                g.tensor_tensor(sq[:], cs[:, :, PAD:], cs[:, :, PAD - w:PAD - w + S], ALU.subtract).then_inc(s["diff_ready"], 1)
                pool.wait_ge(s["diff_ready"], n + 1)
                g.tensor_tensor(sq[:], sq[:], pool_inv[:, n, :].unsqueeze(1).to_broadcast([P, 2, S]), ALU.mult).then_inc(s["diff_scaled"], 1)
                pool.wait_ge(s["diff_scaled"], n + 1)
                g.tensor_tensor(u, sq[:], u, ALU.subtract).then_inc(s["mixed_ready"], 1)
                pool.wait_ge(s["mixed_ready"], n + 1)

            with pool.Fori(0, 4, 1) as it:
                pool.wait_ge(s["hg_values"], it + 1)
                for t in range(2):
                    last = g.tensor_tensor(hg_bd[:, t], hg_i[:, t, :].unsqueeze(1).to_broadcast([P, 4, CH]),
                                           const("chunk_mask").unsqueeze(2).to_broadcast([P, 4, CH]), ALU.mult)
                last.then_inc(s["hg_bd_ready"], 1)
                pool.wait_ge(s["hg_gsig"], it + 1)
                g.tensor_tensor(tmp[:, 1], tmp[:, 1], hg_sg, ALU.mult).then_inc(s["hg_gg0"], 1)
                pool.wait_ge(s["hg_gg0"], it + 1)
                o, _ = PARAMS["hgrn_g"]
                g.tensor_tensor(tmp[:, 1], tmp[:, 1], par[:, bass.ds(it * 2 + o, 2)].unsqueeze(2).to_broadcast([P, 2, S]),
                                ALU.mult).then_inc(s["hg_gg1"], 1)

            out_stage(C_OUT0, "xa0", 0, 0)
            xq_stage(0)
            out_stage(C_OX0, "mix1", 1, 8, heads=0)
            out_stage(C_OUT1, "xa1", 2, 16)
            xq_stage(XA_HEADS)
            out_stage(C_OX1, "final", 3, 24, final=True, heads=XA_HEADS)


def constants():
    import numpy as np
    p = np.arange(P)[:, None]
    j = np.arange(P)[None, :]
    t = np.arange(S)[None, :]
    parts = {
        "ident": p == j,
        "ones": np.ones((P, P)),
        "neg_tri": -1.0 * (p >= j),
        "neg_ones": -np.ones((P, P)),
        "sb_mask": np.concatenate([p < j, np.ones((P, P)), p < j], 1),
        "hg_mask": (p <= j) & (p // HC == j // HC),
        "reset": np.broadcast_to(t % HC != 0, (P, S)),
        "chunk_mask": p // HC == np.arange(P // HC)[None, :],
    }
    inv = np.stack([1.0 / np.minimum(np.arange(1, S + 1), w) for w in WINDOWS])
    return (np.concatenate([np.asarray(parts[n], np.float32) for n in CONSTS], 1),
            np.ascontiguousarray(np.broadcast_to(inv.astype(np.float32), (P, 4, S))))


def kernel(**inputs):
    import numpy as np
    import concourse.bacc as bacc
    from concourse.bass_utils import run_bass_kernel_spmd

    a = {n: np.ascontiguousarray(v) for n, v in inputs.items()}
    tables, inv_count = constants()

    def columns(v):
        return v.reshape(-1, P).T

    rows = {
        "mix0": a["norm_mix_g"][0], "mix1": a["norm_mix_g"][1], "xa0": a["norm_xa_g"][0], "xa1": a["norm_xa_g"][1],
        "mem0": a["norm_mem_g"][0], "mem1": a["norm_mem_g"][1], "final": a["final_norm_g"],
        "pool_scale": a["pool_scale"][0], "bound0": a["hgrn_lower_bounds"][0], "bound1": a["hgrn_lower_bounds"][1],
        "hgrn_g": a["hgrn_norm_g"][0],
    }
    arrays = {
        "x": a["x"], "mem": a["mem"],
        "params": np.ascontiguousarray(np.concatenate([columns(rows[n]) for n in PARAMS], 1)),
        "consts": tables, "inv_count": inv_count, "pool_w": a["pool_w"],
        "w_in_even": a["w_in_even"], "w_out_even": a["w_out_even"], "w_in_odd": a["w_in_odd"],
        "w_out_odd": a["w_out_odd"], "xa_wq": a["xa_wq"], "xa_wkv": a["xa_wkv"], "xa_wo": a["xa_wo"],
    }
    nc = bacc.Bacc("TRN2", target_bir_lowering=False, num_devices=1)
    handles = [nc.dram_tensor(n, v.shape, F32, kind="ExternalInput").ap() for n, v in arrays.items()]
    out = nc.dram_tensor("out", (1, S, D), F32, kind="ExternalOutput").ap()
    build(nc, *handles, out)
    result = run_bass_kernel_spmd(nc, [arrays], core_ids=[0])
    return result.results[0]["out"]
```

```python
from contextlib import ExitStack

import concourse.bass as bass
from concourse import mybir

ALU = mybir.AluOpType
ACT = mybir.ActivationFunctionType
AX = mybir.AxisListType
F32 = mybir.dt.float32
F32R = mybir.dt.float32r

P = 128
D = 2048
S = 256
KT = D // P
CH = 256
NP = 4
KP = KT // NP
EPS = 1e-6
HC = 32
NHC = S // HC
HEAD = 128
XA_HEADS = 4
XA_SCALE = float(D // XA_HEADS) ** -0.5
SB_SCALE = float(HEAD) ** -0.5
WIDTH = D // 2
BIG = 3.0e38
WINDOWS = (2, 4, 8, 16)
PAD = 16

PARAMS = {}
for _name, _n in (("mix0", 16), ("mix1", 16), ("xa0", 16), ("xa1", 16), ("mem0", 16), ("mem1", 16),
                  ("final", 16), ("pool_scale", 8), ("bound0", 8), ("bound1", 8), ("hgrn_g", 8)):
    PARAMS[_name] = (sum(n for _, n in PARAMS.values()), _n)
N_PARAMS = sum(n for _, n in PARAMS.values())

CONSTS = {}
for _name, _n in (("ident", P), ("ones", P), ("neg_tri", P), ("neg_ones", P), ("sb_mask", 3 * P),
                  ("hg_mask", P), ("reset", S), ("chunk_mask", P // HC)):
    CONSTS[_name] = (sum(n for _, n in CONSTS.values()), _n)
N_CONSTS = sum(n for _, n in CONSTS.values())

C_KV0, C_POOL, C_GATE, C_HGRN, C_OUT0, C_XQ0, C_OX0 = 0, 16, 20, 24, 40, 48, 56
C_KV1, C_SB, C_OUT1, C_XQ1, C_OX1, C_END = 64, 80, 112, 120, 128, 136


FINAL_BANK = {(0, 0): 4, (0, 1): 5, (0, 2): 6, (1, 0): 0, (1, 1): 1, (1, 2): 2, (0, 3): 3, (1, 3): 7}
FINAL_ORDER = {rq: n for n, rq in enumerate(FINAL_BANK)}


def build(nc, x, mem, params, consts, inv_count, pool_w, w_in_even, w_out_even, w_in_odd, w_out_odd,
          xa_wq, xa_wkv, xa_wo, out, stop=None):
    with ExitStack() as ctx:
        def sb(name, shape, dt=F32):
            return ctx.enter_context(nc.sbuf_tensor(name, shape, dt))

        def sem(name):
            return ctx.enter_context(nc.semaphore(name))

        raw = sb("raw", [P, NP, KP, CH])
        wpair = sb("wpair", [P, KT, 2, CH], F32R)
        xpair = sb("xpair", [P, KT, 2, S], F32R)
        ypair = sb("ypair", [P, KT, 2, S], F32R)
        xT = sb("xT", [P, KT, S])
        xkT = sb("xkT", [P, KT, S])
        xv = sb("xv", [P, 2, D])
        par = sb("par", [P, N_PARAMS])
        cst = sb("cst", [P, N_CONSTS])
        rs = sb("rs", [P, S + 2])
        acc = sb("acc", [P, 2, S])
        sq = sb("sq", [P, 2, S])
        tmp = sb("tmp", [P, 2, 2, S])
        mrs = sb("mrs", [P, S + 2])
        small = sb("small", [P, 48])
        SCR = 8192
        scratch = sb("scratch", [P, SCR])
        ps = ctx.enter_context(nc.psum_tensor("ps", [P, 8, 512], F32))

        def prm(name, a=0, n=None):
            o, m = PARAMS[name]
            return par[:, o + a:o + a + (n or m)]

        def const(name):
            o, n = CONSTS[name]
            return cst[:, o:o + n]

        def view(off, *shape):
            n = 1
            for s_ in shape:
                n *= s_
            assert off + n <= SCR
            v = scratch[:, off:off + n]
            if len(shape) == 2:
                v = v.rearrange("p (a b) -> p a b", a=shape[0])
            if len(shape) == 3:
                v = v.rearrange("p (a b c) -> p a b c", a=shape[0], b=shape[1])
            return v

        ident, ones = const("ident"), const("ones")
        rs_row = rs[:, 0:S]
        rs_row2 = rs_row.unsqueeze(1).to_broadcast([P, 2, S])
        rs_col = rs[:, S:S + 2]
        rs_col2 = rs_col.unsqueeze(2).to_broadcast([P, 2, S])
        mrs_row2 = mrs[:, 0:S].unsqueeze(1).to_broadcast([P, 2, S])
        mrs_col2 = mrs[:, S:S + 2].unsqueeze(2).to_broadcast([P, 2, S])
        mem_ss, x_ss = small[:, 0:2], small[:, 2:4]
        diag = sq[:, :, 0:P]
        eps = small[:, 10:11]
        xa_negmax, xa_sum, xa_rsum = small[:, 4:6], small[:, 6:8], small[:, 8:10]
        lb, oml = small[:, 16:24], small[:, 24:32]
        lb_t0, lb_t1 = small[:, 32:40], small[:, 40:48]

        x_nat, junk = view(0, 2, D), view(4096, D)
        pool_u, pool_cs = view(0, 8, S), view(2048, 8, PAD + S)
        pool_inv, pool_wt, pool_sig = view(4224, 4, S), view(5248, 4, 2, S), view(7296, 2, S)
        hg_bd = view(0, 2, 4, CH)
        hg_k, hg_b, hg_sg = view(0, 2, S), view(512, 2, S), view(1024, 2, S)
        hg_ke, hg_eb, hg_kt = view(2048, 2, S), view(2560, 2, S), view(3072, 2, S)
        hg_q, hg_ken, hg_i = view(3584, 2, S), view(4096, 4, P), view(4608, 2, S)
        hg_sc, hg_o, hg_sq = view(4096, 4, P), view(5120, 2, S), view(5632, 2, S)
        hg_st = view(6144, 2, NHC - 1, P)
        out_xg = view(7168, 2, S)
        xq_q, xq_e, xq_pt, xq_v = view(0, 4, S), view(1024, 2, S), view(1536, 2, S), view(2048, 2, 512)
        sb_q, sb_k, sb_v, sb_sg = view(0, 2, S), view(512, 2, S), view(1024, 2, S), view(1536, 2, S)
        sb_l, sb_sp, sb_a = view(2048, 2, 3 * P), view(2816, 2, 3 * P), view(3584, 2, 3 * P)

        ident_in, const_in, x_in, pool_in, out_done = (sem(n) for n in ("ident_in", "const_in", "x_in", "pool_in", "out_done"))
        mem_in = [sem(f"mem_in{p}") for p in range(NP)]
        raw_in = [sem(f"raw_in{p}") for p in range(NP)]
        hi_ready = sem("hi_ready")
        lo_ready = sem("lo_ready")
        piece_done = sem("piece_done")
        evac_done = sem("evac_done")
        xpair_ready = sem("xpair_ready")
        ypair_ready = sem("ypair_ready")
        names = """squares_done diag_ready tr_done tr_hi xt_done eps_ready acc_ready acc_zero stats_done rs_raw rs_root rs_ready mem_keys mem_values
            lb_a lb_b lb_c lb_d lb_ready prod_ready cs_ready diff_ready diff_scaled mixed_ready pool_g pool_sig_ready pool_gs pool_mm pool_y
            y_hi hg_logit hg_sig hg_f0 hg_f1 hg_logf hg_bcum hg_exps hg_d hg_kexp hg_keys hg_ktr hg_kcopy hg_values hg_bd_ready
            hg_u hg_state hg_query hg_scores hg_scores_m hg_omm hg_osq hg_norm hg_r0 hg_r1 hg_gate hg_gsig hg_gg0 hg_gg1 hg_y0 hg_y1
            out_tmp x_new x_sq xg_ready xg_hi
            xa_q xa_vcopy xa_scores xa_max xa_exp xa_rs xa_p xa_ptr xa_pt xa_pv xa_hi
            sb_qr sb_kr sb_z sb_abs sb_exp sb_ln sb_sp0 sb_sp1 sb_cum sb_aexp sb_am sb_vr sb_av sb_gate sb_gsig sb_gg sb_y
            fin_tr cs_zero""".split()
        s = {n: sem(n) for n in names}
        fin_out = [[sem(f"fin_out{half}{r}") for r in range(2)] for half in range(2)]

        block = ctx.enter_context(nc.Block())

        def wview(w):
            return w.rearrange("(k p) n -> p k n", p=P)

        W_ine, W_oute, W_ino, W_outo = (wview(w[0]) for w in (w_in_even, w_out_even, w_in_odd, w_out_odd))
        W_q, W_kv, W_o = ([wview(w[l]) for l in range(2)] for w in (xa_wq, xa_wkv, xa_wo))

        @block.sync
        def _(sp):
            def load_chunk(c, w, col):
                for p in range(NP):
                    sp.wait_ge(lo_ready, c * 4 + (p + 1))
                    sp.dma_start(raw[:, p], w[:, KP * p:KP * (p + 1), bass.ds(col, CH)]).then_inc(raw_in[p], 16)

            def plain(c0, w, n_chunks, first=0):
                with sp.Fori(first, n_chunks // 2, 1) as it:
                    for j in range(2):
                        load_chunk(it * 2 + (c0 + j), w, it * (2 * CH) + j * CH)

            mem_v = mem[0].rearrange("(r p) d -> p r d", p=P)
            o, n = CONSTS["ident"]
            assert o == 0

            def load_memory(p):
                cols = slice(p * D // NP, (p + 1) * D // NP)
                sp.dma_start(xv[:, :, cols], mem_v[:, :, cols]).then_inc(mem_in[p], 16)

            def load_piece(c, p, w, col):
                sp.wait_ge(lo_ready, c * 4 + (p + 1))
                sp.dma_start(raw[:, p], w[:, KP * p:KP * (p + 1), col:col + CH]).then_inc(raw_in[p], 16)

            sp.dma_start(cst[:, 0:n], consts[:, 0:n]).then_inc(ident_in, 16)
            sp.dma_start(par[:], params).then_inc(ident_in, 16)
            for p in range(NP):
                load_memory(p)
                load_piece(0, p, W_kv[0], 0)
            sp.dma_start(cst[:, n:], consts[:, n:]).then_inc(const_in, 16)
            load_chunk(1, W_kv[0], CH)
            sp.dma_start(x_nat, x[0].rearrange("(r p) d -> p r d", p=P)).then_inc(x_in, 16)
            plain(C_KV0, W_kv[0], 16, first=1)
            sp.wait_ge(s["squares_done"], 4)
            sp.wait_ge(s["tr_done"], 16)
            sp.dma_start(pool_inv, inv_count).then_inc(pool_in, 16)
            sp.dma_start(pool_wt, pool_w[0].rearrange("g (t p) d -> p (g t) d", p=P)).then_inc(pool_in, 16)
            plain(C_POOL, W_ine, 8)
            with sp.Fori(0, 4, 1) as it:
                for j, base in enumerate((3, 4, 2, 5)):
                    load_chunk(it * 4 + (C_HGRN + j), W_ine, it * CH + base * WIDTH)
            plain(C_OUT0, W_oute, 8)
            plain(C_XQ0, W_q[0], 8)
            plain(C_OX0, W_o[0], 8)
            sp.wait_ge(s["xa_pv"], 2 * XA_HEADS)
            for p in range(NP):
                load_memory(p)
            plain(C_KV1, W_kv[1], 16)
            with sp.Fori(0, 8, 1) as it:
                for j in range(4):
                    load_chunk(it * 4 + (C_SB + j), W_ino, it * CH + j * D)
            plain(C_OUT1, W_outo, 8)
            plain(C_XQ1, W_q[1], 8)
            plain(C_OX1, W_o[1], 8)
            for half in range(2):
                for r in range(2):
                    cols = slice(half * D // 2, (half + 1) * D // 2)
                    sp.wait_ge(fin_out[half][r], 2)
                    sp.dma_start(out[0, r * P:(r + 1) * P, cols], xv[:, r, cols]).then_inc(out_done, 16)
            sp.wait_ge(out_done, 64)

        @block.tensor
        def _(pe):
            mm, tr = nc.tensor.matmul, nc.tensor.transpose

            def piece(c, parity, p, operand, mode, ready=None):
                if p == 0:
                    pe.wait_ge(evac_done, c + 1)
                pe.wait_ge(lo_ready, c * 4 + (p + 5))
                if ready is not None:
                    pe.wait_ge(ready[0], ready[1] + 2 * (p + 1))
                for j in range(2):
                    bank = ps[:, 2 * parity + j, :]
                    for k in range(KP * p, KP * (p + 1)):
                        tile = slice(j * P, (j + 1) * P)
                        still, move = (wpair, operand) if mode == "T" else (operand, wpair)
                        mm(bank, still[:, k, 0, tile], move[:, k].rearrange("p h n -> p (h n)"),
                           start=(k == 0), stop=False)
                        last = mm(bank[:, S:2 * S], still[:, k, 1, tile], move[:, k, 0],
                                  start=False, stop=(k == KT - 1))
                last.then_inc(piece_done, 1)

            def chunk(c, parity, operand, mode, ready=None, hooks=()):
                for p in range(NP):
                    piece(c, parity, p, operand, mode, ready)
                    for at, work in hooks:
                        if at == p:
                            work()

            def transposes(src, batches, landed, free):
                for b in batches:
                    landed(b)
                    if b >= 4:
                        pe.wait_ge(free[0], free[1] + b - 3)
                    for kk in range(2):
                        for r in range(2):
                            k = 2 * b + kk
                            last = tr(ps[:, 4 + b % 4, kk * S + r * P:kk * S + (r + 1) * P],
                                      src[:, r, k * P:(k + 1) * P], ident)
                    last.then_inc(s["tr_done"], 1)

            def spread_sums(n, free):
                pe.wait_ge(s["diag_ready"], n)
                pe.wait_ge(free[0], free[1])
                for r in range(2):
                    last = mm(ps[:, 7, r * P:(r + 1) * P], ones, diag[:, r, :], start=True, stop=True,
                              skip_group_check=True)
                last.then_inc(s["stats_done"], 1)

            def stats(n):
                pe.wait_ge(s["acc_ready"], n)
                bank = ps[:, 7, :]
                for b in range(2):
                    mm(bank[:, 0:S], ones, acc[:, b, :], start=(b == 0), stop=False, skip_group_check=True)
                for r in range(2):
                    for b in range(2):
                        last = mm(bank[:, S + r:S + r + 1], acc[:, b, r * P:(r + 1) * P], ones[:, 0:1],
                                  start=False, stop=(r == 1 and b == 1), skip_group_check=True)
                last.then_inc(s["stats_done"], 1)

            def kv(c0, first=0, ready=None):
                with pe.Fori(first, 4, 1) as it:
                    for j in range(2):
                        chunk(it * 2 + (c0 + j), j, ypair, "T", ready if j == 0 else None)
                with pe.Fori(4, 8, 1) as it:
                    for j in range(2):
                        chunk(it * 2 + (c0 + j), j, ypair, "N")

            def out_stage(c0, ready, heads=None, hooks=()):
                if heads is None:
                    chunk(c0, 0, ypair, "T", ready, hooks)
                else:
                    attend(heads, XA_HEADS - 1, c0, ypair, ready, at=0)
                chunk(c0 + 1, 1, ypair, "T")
                with pe.Fori(1, 4, 1) as it:
                    for j in range(2):
                        chunk(it * 2 + (c0 + j), j, ypair, "T")

            def attend(base, h, c, operand, ready, at):
                n = h + (base + 1)

                def scores():
                    pe.wait_ge(s["xa_q"], n * 2)
                    pe.wait_ge(ypair_ready, h * 2 + (40 if base else 16))
                    for r in range(2):
                        for k in range(4):
                            last = mm(ps[:, 4, r * S:(r + 1) * S], xq_q[:, k, r * P:(r + 1) * P],
                                      xkT[:, bass.ds(h * 4 + k, 1), :].rearrange("p a b -> p (a b)"),
                                      start=(k == 0), stop=(k == 3), skip_group_check=True)
                    last.then_inc(s["xa_scores"], 1)

                def turn():
                    pe.wait_ge(s["xa_p"], n)
                    for m in range(2):
                        for r in range(2):
                            last = tr(ps[:, 5, m * S + r * P:m * S + (r + 1) * P], xq_e[:, r, m * P:(m + 1) * P], ident)
                    last.then_inc(s["xa_ptr"], 1)

                def mix_values():
                    pe.wait_ge(s["xa_pt"], n)
                    pe.wait_ge(s["xa_vcopy"], n)
                    for b in range(4):
                        for m in range(2):
                            last = mm(ps[:, 6 + b // 2, (b % 2) * S:(b % 2 + 1) * S],
                                      xq_v[:, m, b * P:(b + 1) * P], xq_pt[:, m, :],
                                      start=(m == 0), stop=(m == 1), skip_group_check=True)
                        if b % 2:
                            last.then_inc(s["xa_pv"], 1)

                chunk(c, 0, operand, "T", ready, ((at, scores), (at + 1, turn), (at + 2, mix_values)))

            def xq_stage(c0, base, x_ready, n_stats):
                chunk(c0, 0, xpair, "T", x_ready, hooks=((3, lambda: stats(n_stats)),))
                chunk(c0 + 1, 1, xpair, "T")
                with pe.Fori(1, XA_HEADS, 1) as it:
                    attend(base, it - 1, it * 2 + c0, xpair, None, at=1)
                    chunk(it * 2 + (c0 + 1), 1, xpair, "T")

            pe.nop().then_inc(piece_done, 4)
            pe.wait_ge(ident_in, 32)
            transposes(xv, range(8), lambda b: pe.wait_ge(mem_in[b // 2], 16), (ypair_ready, 0))
            chunk(0, 0, ypair, "T", (ypair_ready, 0), ((2, lambda: (
                pe.wait_ge(const_in, 16),
                spread_sums(1, (ypair_ready, 8)))),))
            chunk(1, 1, ypair, "T", hooks=((1, lambda: (
                pe.wait_ge(x_in, 16),
                pe.wait_ge(s["rs_raw"], 1),
                transposes(x_nat, range(0, 4), lambda b: None, None))),))
            chunk(2, 0, ypair, "T", hooks=((1, lambda: transposes(x_nat, range(4, 8), lambda b: None, (xpair_ready, 0))),))
            chunk(3, 1, ypair, "T")
            kv(C_KV0, first=2)
            for c in range(C_POOL, C_GATE):
                chunk(c, c % 2, xpair, "T", hooks=((3, lambda: spread_sums(2, (xpair_ready, 8))),) if c == C_POOL else ())

            def pool_product(g):
                def work():
                    pe.wait_ge(pool_in, 32)
                    pe.wait_ge(s["mixed_ready"], g + 1)
                    if g >= 2:
                        pe.wait_ge(s["pool_y"], 2 * (g - 1))
                    for b in range(2):
                        for t in range(2):
                            last = mm(ps[:, 4 + g % 2, b * S:(b + 1) * S], pool_wt[:, g, t, b * P:(b + 1) * P],
                                      pool_u[:, 2 * g + t, :], start=(t == 0), stop=(t == 1), skip_group_check=True)
                    last.then_inc(s["pool_mm"], 1)
                return work

            for g in range(4):
                chunk(C_GATE + g, g % 2, xpair, "T", hooks=((3, pool_product(g)),))

            def hgrn(it, pipelined):
                def key_transposes():
                    pe.wait_ge(s["hg_keys"], it + 1)
                    for a in range(4):
                        last = tr(ps[:, 4, a * P:(a + 1) * P], hg_ke[:, a // 2, (a % 2) * P:(a % 2 + 1) * P], ident)
                    last.then_inc(s["hg_ktr"], 1)

                def chunk_updates():
                    pe.wait_ge(s["hg_kcopy"], it + 1)
                    pe.wait_ge(s["hg_bd_ready"], it + 1)
                    for a in range(4):
                        h, t = a // 2, a % 2
                        last = mm(ps[:, 4 + a, :], hg_ken[:, a, :], hg_bd[:, t, :, h * P:(h + 1) * P],
                                  start=True, stop=True)
                    last.then_inc(s["hg_u"], 1)

                def intra_scores():
                    pe.wait_ge(s["hg_query"], it + 1)
                    pe.wait_ge(s["hg_state"], it * 14 + 14)
                    for a in range(4):
                        t = slice((a % 2) * P, (a % 2 + 1) * P)
                        last = mm(ps[:, 4, a * P:(a + 1) * P], hg_kt[:, a // 2, t], hg_q[:, a // 2, t],
                                  start=True, stop=True, skip_group_check=True)
                    last.then_inc(s["hg_scores"], 1)

                c = it * 4 + C_HGRN
                chunk(c, 0, xpair, "T", hooks=hgrn_tail(it - 1, 1) if pipelined else ())
                chunk(c + 1, 1, xpair, "N")
                chunk(c + 2, 0, xpair, "T", hooks=((2, key_transposes), (3, chunk_updates)))
                chunk(c + 3, 1, xpair, "T", hooks=((3, intra_scores),))

            def hgrn_tail(it, at):
                def outputs():
                    pe.wait_ge(s["hg_scores_m"], it + 1)
                    for h in range(2):
                        for t in range(2):
                            mm(ps[:, 5, h * S + t * P:h * S + (t + 1) * P], hg_i[:, t, h * P:(h + 1) * P],
                               hg_sc[:, 2 * h + t, :], start=(h == 0 and t == 0), stop=False, skip_group_check=True)
                        for n in range(1, NHC):
                            last = mm(ps[:, 5, h * S + n * HC:h * S + (n + 1) * HC], hg_st[:, h, n - 1, :],
                                      hg_q[:, h, n * HC:(n + 1) * HC], start=False,
                                      stop=(h == 1 and n == NHC - 1), skip_group_check=True)
                    last.then_inc(s["hg_omm"], 1)

                def head_norm():
                    pe.wait_ge(s["hg_osq"], it + 1)
                    mm(ps[:, 6, :], ones, hg_sq.rearrange("p a b -> p (a b)"),
                       start=True, stop=True).then_inc(s["hg_norm"], 1)

                return ((at, outputs), (at + 1, head_norm))

            hgrn(0, False)
            with pe.Fori(1, 4, 1) as it:
                hgrn(it, True)

            out_stage(C_OUT0, (ypair_ready, 8), hooks=hgrn_tail(3, 0))
            xq_stage(C_XQ0, 0, (xpair_ready, 8), 1)
            out_stage(C_OX0, (ypair_ready, 16), heads=0)
            transposes(xv, range(8), lambda b: pe.wait_ge(mem_in[b // 2], 32), (ypair_ready, 24))
            chunk(C_KV1, 0, ypair, "T", (ypair_ready, 24), hooks=((2, lambda: (
                pe.wait_ge(ypair_ready, 32),
                stats(2))),))
            chunk(C_KV1 + 1, 1, ypair, "T")
            kv(C_KV1, first=1)

            with pe.Fori(0, 8, 1) as it:
                def logits():
                    pe.wait_ge(s["sb_kr"], it + 1)
                    for h in range(2):
                        mm(ps[:, 4 + h, 0:S], sb_k[:, h, 0:P], sb_q[:, h, :],
                           start=True, stop=False, skip_group_check=True)
                        mm(ps[:, 4 + h, S:S + P], sb_k[:, h, P:S], sb_q[:, h, P:S],
                           start=False, stop=False, skip_group_check=True).then_inc(s["sb_z"], 1)

                def cumulate():
                    for h in range(2):
                        pe.wait_ge(s["sb_sp1"], it * 2 + (h + 1))
                        bank = ps[:, 4 + h, :]
                        mm(bank[:, 0:S], const("neg_tri"), sb_sp[:, h, 0:S], start=False, stop=False, skip_group_check=True)
                        mm(bank[:, P:S], const("neg_ones"), sb_sp[:, h, S:S + P], start=False, stop=False, skip_group_check=True)
                        mm(bank[:, S:S + P], const("neg_tri"), sb_sp[:, h, S:S + P], start=False, stop=True,
                           skip_group_check=True).then_inc(s["sb_cum"], 1)

                def mix_values():
                    pe.wait_ge(s["sb_vr"], it + 1)
                    pe.wait_ge(s["sb_am"], it * 2 + 2)
                    for h in range(2):
                        v = slice(h * P, (h + 1) * P)
                        mm(ps[:, 6, h * S:(h + 1) * S], sb_v[:, 0, v], sb_a[:, h, 0:S],
                           start=(h == 0), stop=False, skip_group_check=True)
                        last = mm(ps[:, 6, h * S + P:(h + 1) * S], sb_v[:, 1, v], sb_a[:, h, S:S + P],
                                  start=False, stop=(h == 1), skip_group_check=True)
                    last.then_inc(s["sb_av"], 1)

                c = it * 4 + C_SB
                chunk(c, 0, xpair, "T", (xpair_ready, 16))
                chunk(c + 1, 1, xpair, "T")
                chunk(c + 2, 0, xpair, "N", hooks=((1, logits),))
                chunk(c + 3, 1, xpair, "T", hooks=((0, cumulate), (2, mix_values)))

            out_stage(C_OUT1, (ypair_ready, 32))
            xq_stage(C_XQ1, XA_HEADS, (xpair_ready, 24), 3)
            out_stage(C_OX1, (ypair_ready, 40), heads=XA_HEADS)
            def transpose_block(r, q):
                for k in range(4 * q, 4 * q + 4):
                    last = tr(ps[:, FINAL_BANK[r, q], (k % 4) * P:(k % 4 + 1) * P], xkT[:, k, r * P:(r + 1) * P], ident)
                last.then_inc(s["fin_tr"], 1)

            pe.wait_ge(s["xg_ready"], 24 + 6)
            pe.wait_ge(evac_done, C_END + 1)
            for q in range(3):
                transpose_block(0, q)
            for q in range(2):
                transpose_block(1, q)
            pe.wait_ge(evac_done, C_END + 2)
            transpose_block(1, 2)
            pe.wait_ge(s["acc_ready"], 4)
            pe.wait_ge(s["x_sq"], 24 + 8)
            for r in range(2):
                for n, part in enumerate((acc, sq)):
                    for b in range(2):
                        last = mm(ps[:, 7, S + r:S + r + 1], part[:, b, r * P:(r + 1) * P], ones[:, 0:1],
                                  start=(r == n == b == 0), stop=(r == n == b == 1), skip_group_check=True)
            last.then_inc(s["stats_done"], 1)
            pe.wait_ge(s["xg_ready"], 24 + 8)
            transpose_block(0, 3)
            pe.wait_ge(s["rs_raw"], 6)
            transpose_block(1, 3)

        @block.scalar
        def _(act):
            fn = nc.scalar.activation

            def split_hi(c, p):
                act.wait_ge(raw_in[p], c * 16 + 16)
                act.wait_ge(piece_done, c * 4 + (p + 1))
                fn(wpair[:, KP * p:KP * (p + 1), 0, :], raw[:, p], ACT.Copy).then_inc(hi_ready, 1)

            def slot(c, steps=(), convert=True):
                for p in range(NP):
                    if convert:
                        split_hi(c + 1, p)
                    for at, work in steps:
                        if at == p:
                            work()

            def rs_root(n, dst=rs):
                act.wait_ge(s["rs_raw"], n)
                fn(dst[:, :], dst[:, :], ACT.Sqrt).then_inc(s["rs_root"], 1)

            def squares(n, src, sums):
                for r in range(2):
                    if n + r:
                        act.wait_ge(s["squares_done"], n + r)
                    fn(junk, src[:, r, :], ACT.Square, accum_out=sums[:, r:r + 1]).then_inc(s["squares_done"], 1)

            def transposed_x(batches):
                for b in batches:
                    act.wait_ge(s["tr_done"], 8 + b + 1)
                    fn(xT[:, 2 * b:2 * b + 2, :], ps[:, 4 + b % 4, :].rearrange("p (a b) -> p a b", a=2), ACT.Copy)
                    for kk in range(2):
                        last = fn(xpair[:, 2 * b + kk, 0, :], ps[:, 4 + b % 4, kk * S:(kk + 1) * S], ACT.Copy,
                                  scale=prm("mix0", 2 * b + kk, 1))
                    last.then_inc(s["tr_hi"], 1)

            def transposed_mem(gain, tr0):
                for b in range(8):
                    act.wait_ge(s["tr_done"], tr0 + b + 1)
                    for kk in range(2):
                        last = fn(ypair[:, 2 * b + kk, 0, :], ps[:, 4 + b % 4, kk * S:(kk + 1) * S], ACT.Copy,
                                  scale=prm(gain, 2 * b + kk, 1))
                    last.then_inc(s["tr_hi"], 1)

            def out_stage(c0, heads=None, pair=True, steps=(), after=None):
                def hi(it, j):
                    def work():
                        act.wait_ge(s["xg_ready"], n_xg + it * 2 + (j + 1))
                        k = it * 4 + 2 * j
                        fn(xpair[:, bass.ds(k, 2), 0, :], out_xg, ACT.Copy).then_inc(s["xg_hi"], 1)
                    return work
                n_xg = xg_count[0]
                xg_count[0] += 8
                if heads is not None:
                    steps = attend(heads, XA_HEADS - 1, at=0)
                slot(c0, steps + (((3, hi(0, 0)),) if pair else ()))
                slot(c0 + 1, ((3, hi(0, 1)),) if pair else ())
                with act.Fori(1, 4 if after is None else 3, 1) as it:
                    for j in range(2):
                        slot(it * 2 + (c0 + j), ((3, hi(it, j)),) if pair else ())
                if after is not None:
                    slot(c0 + 6, ((3, hi(3, 0)),) if pair else ())
                    slot(c0 + 7, ((3, after),) + (((3, hi(3, 1)),) if pair else ()), convert=c0 + 8 < C_END)

            xg_count = [0]

            def attend(base, h, at):
                n = h + (base + 1)

                def exps():
                    act.wait_ge(s["xa_max"], n)
                    for r in range(2):
                        last = fn(xq_e[:, r, :], ps[:, 4, r * S:(r + 1) * S], ACT.Exp,
                                  bias=xa_negmax[:, r:r + 1], accum_out=xa_sum[:, r:r + 1])
                    last.then_inc(s["xa_exp"], 1)

                def copy_pt():
                    act.wait_ge(s["xa_ptr"], n)
                    fn(xq_pt.rearrange("p a b -> p (a b)"), ps[:, 5, :], ACT.Copy).then_inc(s["xa_pt"], 1)

                def hi():
                    for b in range(2):
                        act.wait_ge(s["xa_pv"], n * 2 + (b - 1))
                        fn(ypair[:, bass.ds(h * 4 + 2 * b, 2), 0, :],
                           ps[:, 6 + b, :].rearrange("p (a b) -> p a b", a=2), ACT.Copy).then_inc(s["xa_hi"], 1)
                return ((at, exps), (at + 1, copy_pt), (at + 2, hi))

            def xq_stage(c0, base, n_stats):
                slot(c0, ((3, lambda: rs_root(n_stats)),))
                slot(c0 + 1)
                with act.Fori(1, XA_HEADS, 1) as it:
                    slot(it * 2 + c0, attend(base, it - 1, at=1))
                    slot(it * 2 + (c0 + 1))

            act.wait_ge(s["eps_ready"], 1)
            act.wait_ge(ident_in, 32)
            split_hi(0, 0)
            transposed_mem("mem0", 0)
            for p in range(1, NP):
                split_hi(0, p)
            squares(0, xv, mem_ss)
            slot(0, ((3, lambda: rs_root(1, mrs)),))

            def bounds():
                act.wait_ge(s["lb_a"], 2)
                fn(lb_t0, lb_t0, ACT.Exp)
                fn(lb_t1, lb_t1, ACT.Exp).then_inc(s["lb_b"], 1)

            slot(1, ((2, lambda: transposed_x(range(0, 4))),))
            slot(2, ((2, lambda: transposed_x(range(4, 8))), (3, lambda: squares(2, x_nat, x_ss))))
            slot(3)
            with act.Fori(2, C_POOL // 2, 1) as it:
                for j in range(2):
                    slot(it * 2 + j)
            bounds()
            for c in range(C_POOL, C_GATE):
                slot(c, ((3, lambda: rs_root(2)),) if c == C_POOL else ())
            for g in range(4):
                def gate_sigmoid():
                    act.wait_ge(s["pool_g"], g + 1)
                    fn(pool_sig, tmp[:, g % 2], ACT.Sigmoid).then_inc(s["pool_sig_ready"], 1)
                    act.wait_ge(s["pool_y"], 2 * (g + 1))
                    fn(ypair[:, 2 * g:2 * g + 2, 0, :], tmp[:, g % 2], ACT.Copy).then_inc(s["y_hi"], 1)
                slot(C_GATE + g, ((3, gate_sigmoid),))

            def hgrn(it, pipelined):
                def sigmoid():
                    act.wait_ge(s["hg_logit"], it + 1)
                    fn(hg_k, hg_k, ACT.Sigmoid).then_inc(s["hg_sig"], 1)

                def log_f():
                    nc.scalar.preload_act_table_set("natural_log_exp_and_others")
                    act.wait_ge(s["hg_f1"], it + 1)
                    fn(hg_ke, hg_k, ACT.Ln).then_inc(s["hg_logf"], 1)

                def exps():
                    act.wait_ge(s["hg_bcum"], it + 1)
                    fn(hg_eb, hg_b, ACT.Exp)
                    fn(hg_kt, hg_b, ACT.Exp, scale=-1.0).then_inc(s["hg_exps"], 1)

                def key_exp():
                    act.wait_ge(s["hg_d"], it + 1)
                    fn(hg_ke, hg_ke, ACT.Exp).then_inc(s["hg_kexp"], 1)

                def key_copy():
                    act.wait_ge(s["hg_ktr"], it + 1)
                    fn(hg_ken.rearrange("p a b -> p (a b)"), ps[:, 4, :], ACT.Copy).then_inc(s["hg_kcopy"], 1)

                def gate():
                    act.wait_ge(s["hg_gate"], it + 1)
                    fn(hg_sg, tmp[:, 1], ACT.Sigmoid).then_inc(s["hg_gsig"], 1)

                c = it * 4 + C_HGRN
                slot(c, (hgrn_tail(it - 1, 1) if pipelined else ()) + ((3, sigmoid),))
                slot(c + 1, ((1, log_f), (2, exps), (3, key_exp)))
                slot(c + 2, ((2, key_copy),))
                slot(c + 3, ((3, gate),))

            def hgrn_tail(it, at):
                def output_squares():
                    nc.scalar.preload_act_table_set("natural_log_exp_and_others")
                    act.wait_ge(s["hg_omm"], it + 1)
                    o = ps[:, 5, :].rearrange("p (a b) -> p a b", a=2)
                    fn(hg_sq, o, ACT.Square)
                    fn(hg_o, o, ACT.Copy).then_inc(s["hg_osq"], 1)

                def norm_factor():
                    act.wait_ge(s["hg_norm"], it + 1)
                    fn(hg_ke, ps[:, 6, :].rearrange("p (a b) -> p a b", a=2), ACT.Ln, scale=1.0 / HEAD,
                       bias=eps).then_inc(s["hg_r0"], 1)
                    act.wait_ge(s["hg_r0"], it + 1)
                    fn(hg_ke, hg_ke, ACT.Exp, scale=-0.5).then_inc(s["hg_r1"], 1)
                    act.wait_ge(s["hg_y1"], it + 1)
                    fn(ypair[:, bass.ds(it * 2 + 8, 2), 0, :], hg_o, ACT.Copy).then_inc(s["y_hi"], 1)
                return ((at, output_squares), (at + 1, norm_factor))

            hgrn(0, False)
            with act.Fori(1, 4, 1) as it:
                hgrn(it, True)

            out_stage(C_OUT0, steps=hgrn_tail(3, 0))
            xq_stage(C_XQ0, 0, 3)
            out_stage(C_OX0, heads=0, after=lambda: transposed_mem("mem1", 16))
            slot(C_KV1, ((3, lambda: rs_root(4)),))
            slot(C_KV1 + 1)
            with act.Fori(1, 8, 1) as it:
                for j in range(2):
                    slot(it * 2 + (C_KV1 + j))

            with act.Fori(0, 8, 1) as it:
                def softplus():
                    nc.scalar.preload_act_table_set("natural_log_exp_and_others")
                    for h in range(2):
                        act.wait_ge(s["sb_z"], it * 2 + (h + 1))
                        fn(sb_l[:, h, :], ps[:, 4 + h, 0:3 * P], ACT.Abs).then_inc(s["sb_abs"], 1)
                    for h in range(2):
                        act.wait_ge(s["sb_abs"], it * 2 + (h + 1))
                        fn(sb_l[:, h, :], sb_l[:, h, :], ACT.Exp, scale=-1.0).then_inc(s["sb_exp"], 1)
                    for h in range(2):
                        act.wait_ge(s["sb_exp"], it * 2 + (h + 1))
                        fn(sb_l[:, h, :], sb_l[:, h, :], ACT.Ln, bias=1.0).then_inc(s["sb_ln"], 1)

                def weights():
                    for h in range(2):
                        act.wait_ge(s["sb_cum"], it * 2 + (h + 1))
                        fn(sb_a[:, h, :], ps[:, 4 + h, 0:3 * P], ACT.Exp).then_inc(s["sb_aexp"], 1)

                def gate():
                    act.wait_ge(s["sb_gate"], it + 1)
                    fn(sb_sg, tmp[:, 1], ACT.Sigmoid).then_inc(s["sb_gsig"], 1)
                    act.wait_ge(s["sb_y"], it + 1)
                    fn(ypair[:, bass.ds(it * 2, 2), 0, :], tmp[:, 1], ACT.Copy).then_inc(s["y_hi"], 1)

                c = it * 4 + C_SB
                slot(c)
                slot(c + 1)
                slot(c + 2, ((1, softplus),))
                slot(c + 3, ((0, weights), (3, gate)))

            out_stage(C_OUT1)
            xq_stage(C_XQ1, XA_HEADS, 5)
            def last_squares():
                act.wait_ge(s["xt_done"], 24 + 7)
                act.wait_ge(s["x_new"], 24 + 8)
                fn(sq[:], xT[:, KT - 2:KT, :], ACT.Square).then_inc(s["x_sq"], 1)

            out_stage(C_OX1, heads=XA_HEADS, pair=False, after=last_squares)
            act.wait_ge(s["rs_raw"], 6)
            fn(rs_col, rs_col, ACT.Sqrt).then_inc(s["rs_root"], 1)
            act.wait_ge(s["rs_ready"], 6)
            for half in range(2):
                for r in range(2):
                    q = 2 * half
                    act.wait_ge(s["fin_tr"], FINAL_ORDER[r, q] + 1)
                    fn(xv[:, r, q * 512:(q + 1) * 512], ps[:, FINAL_BANK[r, q], :], ACT.Copy,
                       scale=rs_col[:, r:r + 1]).then_inc(fin_out[half][r], 1)

        @block.vector
        def _(dve):
            v = nc.vector
            END = "end"

            def split_lo(c, p):
                dve.wait_ge(hi_ready, c * 4 + (p + 1))
                kp = slice(KP * p, KP * (p + 1))
                v.tensor_tensor(wpair[:, kp, 1, :], raw[:, p], wpair[:, kp, 0, :].bitcast(F32),
                                ALU.subtract).then_inc(lo_ready, 1)

            def slot(c, steps=(), convert=True):
                for p in range(NP):
                    for at, work in steps:
                        if at == END and p == NP - 1:
                            work()
                    if convert:
                        split_lo(c + 1, p)
                    for at, work in steps:
                        if at == p:
                            work()

            def take(c, parity, dst):
                dve.wait_ge(piece_done, c * 4 + 8)
                v.tensor_reduce(dst, ps[:, 2 * parity:2 * parity + 2, :].rearrange("p j (h n) -> p j n h", h=2),
                                AX.X, ALU.add).then_inc(evac_done, 1)
                dve.wait_ge(evac_done, c + 3)

            def rs_step(n, dst=rs, sums=None):
                dve.wait_ge(s["stats_done"], n)
                width = S if sums is not None else S + 2
                if sums is not None:
                    v.tensor_scalar(dst[:, S:S + 2], sums, 1.0 / D, EPS, ALU.mult, ALU.add)
                v.tensor_scalar(dst[:, 0:width], ps[:, 7, 0:width], 1.0 / D, EPS, ALU.mult, ALU.add).then_inc(s["rs_raw"], 1)
                dve.wait_ge(s["rs_root"], n)
                v.reciprocal(dst[:, :], dst[:, :]).then_inc(s["rs_ready"], 1)
                dve.wait_ge(s["rs_ready"], n)

            def diagonal(n, sums):
                dve.wait_ge(s["squares_done"], 2 * n)
                if n > 1:
                    dve.wait_ge(s["stats_done"], n - 1)
                for r in range(2):
                    last = v.tensor_scalar(diag[:, r, :], ident, sums[:, r:r + 1], None, ALU.mult)
                last.then_inc(s["diag_ready"], 1)

            def transposed_lo(dst, gain, hi0, done, batches=range(8)):
                for b in batches:
                    dve.wait_ge(s["tr_hi"], hi0 + b + 1)
                    for kk in range(2):
                        k = 2 * b + kk
                        last = v.scalar_tensor_tensor(dst[:, k, 1, :], ps[:, 4 + b % 4, kk * S:(kk + 1) * S],
                                                      prm(gain, k, 1), dst[:, k, 0, :].bitcast(F32),
                                                      ALU.mult, ALU.subtract)
                    last.then_inc(done, 1)

            def keys(c0, it, j):
                def work():
                    take(it * 2 + (c0 + j), j, tmp[:, j])
                    v.tensor_tensor(xkT[:, bass.ds(it * 4 + 2 * j, 2), :], tmp[:, j], mrs_row2, ALU.mult).then_inc(s["mem_keys"], 1)
                return work

            def kv(c0, first):
                with dve.Fori(first, 4, 1) as it:
                    for j in range(2):
                        slot(it * 2 + (c0 + j), ((END, keys(c0, it, j)),))
                with dve.Fori(0, 4, 1) as it:
                    for j in range(2):
                        def values():
                            take(it * 2 + (c0 + 8 + j), j, tmp[:, j])
                            v.tensor_tensor(xv[:, :, bass.ds(it * (2 * CH) + j * CH, CH)], tmp[:, j], mrs_col2,
                                            ALU.mult).then_inc(s["mem_values"], 1)
                        slot(it * 2 + (c0 + 8 + j), ((END, values),))

            def attend(base, h, at):
                n = h + (base + 1)

                def softmax():
                    dve.wait_ge(s["xa_scores"], n)
                    v.tensor_reduce(xa_negmax, ps[:, 4, :].rearrange("p (a b) -> p a b", a=2), AX.X, ALU.max,
                                    negate=True).then_inc(s["xa_max"], 1)
                    dve.wait_ge(s["xa_exp"], n)
                    v.reciprocal(xa_rsum, xa_sum).then_inc(s["xa_rs"], 1)
                    dve.wait_ge(s["xa_rs"], n)
                    for r in range(2):
                        last = v.tensor_scalar(xq_e[:, r, :], xq_e[:, r, :], xa_rsum[:, r:r + 1], None, ALU.mult)
                    last.then_inc(s["xa_p"], 1)

                def lo():
                    for b in range(2):
                        dve.wait_ge(s["xa_hi"], n * 2 + (b - 1))
                        v.tensor_tensor(ypair[:, bass.ds(h * 4 + 2 * b, 2), 1, :],
                                        ps[:, 6 + b, :].rearrange("p (a b) -> p a b", a=2),
                                        ypair[:, bass.ds(h * 4 + 2 * b, 2), 0, :].bitcast(F32),
                                        ALU.subtract).then_inc(ypair_ready, 1)
                return ((at, softmax), (at + 2, lo))

            def xq_stage(c0, base, n_stats):
                def query(it, j):
                    def work():
                        take(it * 2 + (c0 + j), j, tmp[:, j])
                        v.scalar_tensor_tensor(xq_q[:, 2 * j:2 * j + 2, :], tmp[:, j], XA_SCALE, rs_row2,
                                               ALU.mult, ALU.mult).then_inc(s["xa_q"], 1)
                    return work
                slot(c0, ((3, lambda: rs_step(n_stats)), (3, query(0, 0))))
                slot(c0 + 1, ((END, query(0, 1)),))
                with dve.Fori(1, XA_HEADS, 1) as it:
                    slot(it * 2 + c0, attend(base, it - 1, at=1) + ((END, query(it, 0)),))
                    slot(it * 2 + (c0 + 1), ((END, query(it, 1)),))

            out_count = [0]

            def out_stage(c0, heads=None, pair=True, steps=(), after=None):
                n0 = out_count[0]
                out_count[0] += 8

                def residual(it, j):
                    def take_product():
                        if not pair:
                            dve.wait_ge(s["x_new"], n0 + it * 2 + (j - 1))
                        take(it * 2 + (c0 + j), j, tmp[:, j])
                        v.nop().then_inc(s["out_tmp"], 1)

                    def lo():
                        dve.wait_ge(s["xg_hi"], n0 + it * 2 + (j + 1))
                        v.tensor_tensor(xpair[:, bass.ds(it * 4 + 2 * j, 2), 1, :], out_xg,
                                        xpair[:, bass.ds(it * 4 + 2 * j, 2), 0, :].bitcast(F32),
                                        ALU.subtract).then_inc(xpair_ready, 1)
                    return ((END, take_product),) + (((3, lo),) if pair else ())
                if heads is not None:
                    steps = attend(heads, XA_HEADS - 1, at=0)
                slot(c0, steps + residual(0, 0))
                slot(c0 + 1, residual(0, 1))
                with dve.Fori(1, 4 if after is None else 3, 1) as it:
                    for j in range(2):
                        slot(it * 2 + (c0 + j), residual(it, j))
                if after is not None:
                    slot(c0 + 6, residual(3, 0))
                    slot(c0 + 7, ((3, after),) + residual(3, 1), convert=c0 + 8 < C_END)

            v.memset(eps, EPS).then_inc(s["eps_ready"], 1)
            v.nop().then_inc(lo_ready, 4)
            v.nop().then_inc(evac_done, 2)
            dve.wait_ge(ident_in, 32)
            split_lo(0, 0)
            transposed_lo(ypair, "mem0", 0, ypair_ready)
            for p in range(1, NP):
                split_lo(0, p)
            diagonal(1, mem_ss)
            slot(0, ((3, lambda: rs_step(1, mrs, mem_ss)), (3, keys(0, 0, 0))))
            slot(1, ((2, lambda: transposed_lo(xpair, "mix0", 8, xpair_ready, range(0, 4))), (END, keys(0, 0, 1))))
            slot(2, ((2, lambda: transposed_lo(xpair, "mix0", 8, xpair_ready, range(4, 8))), (END, keys(0, 1, 0))))
            slot(3, ((END, keys(0, 1, 1)),))
            v.tensor_tensor(lb, prm("bound0"), prm("bound1"), ALU.max).then_inc(s["lb_a"], 1)
            dve.wait_ge(s["lb_a"], 1)
            v.tensor_tensor(lb_t0, prm("bound0"), lb, ALU.subtract)
            v.tensor_tensor(lb_t1, prm("bound1"), lb, ALU.subtract).then_inc(s["lb_a"], 1)
            kv(C_KV0, first=2)
            dve.wait_ge(s["lb_b"], 1)
            v.tensor_tensor(lb_t1, lb_t0, lb_t1, ALU.add).then_inc(s["lb_c"], 1)
            dve.wait_ge(s["lb_c"], 1)
            v.reciprocal(lb_t1, lb_t1).then_inc(s["lb_c"], 1)
            dve.wait_ge(s["lb_c"], 2)
            v.tensor_tensor(lb, lb_t0, lb_t1, ALU.mult).then_inc(s["lb_d"], 1)
            dve.wait_ge(s["lb_d"], 1)
            v.tensor_scalar(oml, lb, -1.0, 1.0, ALU.mult, ALU.add).then_inc(s["lb_ready"], 1)

            for c in range(C_POOL, C_GATE):
                def pool_input():
                    b = 2 * (c - C_POOL)
                    take(c, c % 2, tmp[:, c % 2])
                    v.tensor_tensor(pool_u[:, b:b + 2, :], tmp[:, c % 2], rs_row2, ALU.mult).then_inc(s["prod_ready"], 1)
                    dve.wait_ge(s["prod_ready"], c - C_POOL + 1)
                    if c == C_POOL:
                        dve.wait_ge(s["cs_zero"], 1)
                    for k in range(b, b + 2):
                        last = v.tensor_tensor_scan(pool_cs[:, k, PAD:], ones[:, 0:1].to_broadcast([P, S]),
                                                    pool_u[:, k, :], 0.0, ALU.mult, ALU.add)
                    last.then_inc(s["cs_ready"], 1)
                if c == C_POOL:
                    slot(c, ((0, lambda: diagonal(2, x_ss)), (3, lambda: rs_step(2, rs, x_ss)), (3, pool_input)))
                else:
                    slot(c, ((END, pool_input),))
            for g in range(4):
                def pool_gate():
                    t = tmp[:, g % 2]
                    take(C_GATE + g, g % 2, t)
                    v.tensor_tensor(t, t, rs_row2, ALU.mult).then_inc(s["pool_g"], 1)

                def pool_output():
                    t = tmp[:, g % 2]
                    dve.wait_ge(s["pool_sig_ready"], g + 1)
                    v.tensor_tensor(t, t, pool_sig, ALU.mult).then_inc(s["pool_gs"], 1)
                    dve.wait_ge(s["pool_gs"], g + 1)
                    dve.wait_ge(s["pool_mm"], g + 1)
                    for b in range(2):
                        v.scalar_tensor_tensor(t[:, b, :], ps[:, 4 + g % 2, b * S:(b + 1) * S],
                                               prm("pool_scale", 2 * g + b, 1), t[:, b, :],
                                               ALU.mult, ALU.mult).then_inc(s["pool_y"], 1)
                    dve.wait_ge(s["y_hi"], g + 1)
                    v.tensor_tensor(ypair[:, 2 * g:2 * g + 2, 1, :], t, ypair[:, 2 * g:2 * g + 2, 0, :].bitcast(F32),
                                    ALU.subtract).then_inc(ypair_ready, 1)
                slot(C_GATE + g, ((END, pool_gate), (3, pool_output)))

            def hgrn(it, pipelined):
                c = it * 4 + C_HGRN

                def bc(ap):
                    return ap.unsqueeze(2).to_broadcast([P, 2, S])

                def logits():
                    take(c, 0, tmp[:, 0])
                    v.tensor_tensor(hg_k, tmp[:, 0], rs_row2, ALU.mult).then_inc(s["hg_logit"], 1)

                def forget():
                    dve.wait_ge(s["hg_sig"], it + 1)
                    v.tensor_tensor(hg_k, hg_k, bc(oml[:, bass.ds(it * 2, 2)]), ALU.mult).then_inc(s["hg_f0"], 1)
                    dve.wait_ge(s["hg_f0"], it + 1)
                    v.tensor_tensor(hg_k, hg_k, bc(lb[:, bass.ds(it * 2, 2)]), ALU.add).then_inc(s["hg_f1"], 1)

                def cumulate():
                    dve.wait_ge(s["hg_logf"], it + 1)
                    for h in range(2):
                        last = v.tensor_tensor_scan(hg_b[:, h, :], const("reset"), hg_ke[:, h, :], 0.0, ALU.mult, ALU.add)
                    last.then_inc(s["hg_bcum"], 1)
                    v.tensor_scalar(hg_k, hg_k, -1.0, 1.0, ALU.mult, ALU.add)

                def key_exponent():
                    b4 = hg_b.rearrange("p a (n c) -> p (a n) c", c=HC)
                    dve.wait_ge(s["hg_bcum"], it + 1)
                    v.tensor_tensor(hg_ke.rearrange("p a (n c) -> p (a n) c", c=HC),
                                    b4[:, :, HC - 1:HC].to_broadcast([P, 2 * NHC, HC]), b4,
                                    ALU.subtract).then_inc(s["hg_d"], 1)

                def keys():
                    dve.wait_ge(s["hg_kexp"], it + 1)
                    dve.wait_ge(s["hg_exps"], it + 1)
                    v.tensor_tensor(hg_kt, hg_kt, hg_k, ALU.mult)
                    v.tensor_tensor(hg_ke, hg_ke, hg_k, ALU.mult).then_inc(s["hg_keys"], 1)

                def values():
                    take(c + 1, 1, tmp[:, 1])
                    v.tensor_tensor(hg_i, tmp[:, 1], rs_col2, ALU.mult).then_inc(s["hg_values"], 1)

                def states():
                    dve.wait_ge(s["hg_u"], it + 1)
                    for n in range(NHC - 1):
                        for h in range(2):
                            u = ps[:, 4 + 2 * h + n // 4, (n % 4) * P:(n % 4 + 1) * P]
                            if n == 0:
                                v.tensor_copy(hg_st[:, h, 0, :], u).then_inc(s["hg_state"], 1)
                                continue
                            at = n * HC + HC - 1
                            dve.wait_ge(s["hg_state"], it * 14 + (2 * (n - 1) + h + 1))
                            v.scalar_tensor_tensor(hg_st[:, h, n, :], hg_st[:, h, n - 1, :], hg_eb[:, h, at:at + 1], u,
                                                   ALU.mult, ALU.add).then_inc(s["hg_state"], 1)

                def queries():
                    take(c + 2, 0, tmp[:, 0])
                    v.tensor_tensor(hg_q, tmp[:, 0], rs_row2, ALU.mult).then_inc(s["prod_ready"], 1)
                    dve.wait_ge(s["prod_ready"], it + 5)
                    v.tensor_tensor(hg_q, hg_q, hg_eb, ALU.mult).then_inc(s["hg_query"], 1)

                def mask_scores():
                    dve.wait_ge(s["hg_scores"], it + 1)
                    v.tensor_tensor(hg_sc, ps[:, 4, :].rearrange("p (a b) -> p a b", a=4),
                                    const("hg_mask").unsqueeze(1).to_broadcast([P, 4, P]), ALU.mult).then_inc(s["hg_scores_m"], 1)

                def gate():
                    take(c + 3, 1, tmp[:, 1])
                    v.tensor_tensor(tmp[:, 1], tmp[:, 1], rs_row2, ALU.mult).then_inc(s["hg_gate"], 1)

                slot(c, (hgrn_tail(it - 1, 1) if pipelined else ()) + ((END, logits),))
                slot(c + 1, ((0, forget), (1, cumulate), (2, key_exponent), (END, values), (3, keys)))
                slot(c + 2, ((END, queries),))
                slot(c + 3, ((0, states), (END, gate), (3, mask_scores)))

            def hgrn_tail(it, at):
                def finish():
                    dve.wait_ge(s["hg_r1"], it + 1)
                    v.tensor_tensor(hg_o, hg_o, hg_ke, ALU.mult).then_inc(s["hg_y0"], 1)
                    dve.wait_ge(s["hg_y0"], it + 1)
                    dve.wait_ge(s["hg_gg1"], it + 1)
                    v.tensor_tensor(hg_o, hg_o, tmp[:, 1], ALU.mult).then_inc(s["hg_y1"], 1)
                    dve.wait_ge(s["y_hi"], it + 5)
                    v.tensor_tensor(ypair[:, bass.ds(it * 2 + 8, 2), 1, :], hg_o,
                                    ypair[:, bass.ds(it * 2 + 8, 2), 0, :].bitcast(F32), ALU.subtract).then_inc(ypair_ready, 1)
                return ((at + 1, finish),)

            hgrn(0, False)
            with dve.Fori(1, 4, 1) as it:
                hgrn(it, True)

            out_stage(C_OUT0, steps=hgrn_tail(3, 0))
            xq_stage(C_XQ0, 0, 3)
            out_stage(C_OX0, heads=0, after=lambda: transposed_lo(ypair, "mem1", 16, ypair_ready))
            slot(C_KV1, ((3, lambda: rs_step(4)), (3, keys(C_KV1, 0, 0))))
            slot(C_KV1 + 1, ((END, keys(C_KV1, 0, 1)),))
            kv(C_KV1, first=1)

            with dve.Fori(0, 8, 1) as it:
                c = it * 4 + C_SB

                def queries():
                    take(c, 0, tmp[:, 0])
                    v.scalar_tensor_tensor(sb_q, tmp[:, 0], SB_SCALE, rs_row2, ALU.mult, ALU.mult).then_inc(s["sb_qr"], 1)

                def keys():
                    take(c + 1, 1, tmp[:, 1])
                    v.tensor_tensor(sb_k, tmp[:, 1], rs_row2, ALU.mult).then_inc(s["sb_kr"], 1)

                def softplus():
                    for h in range(2):
                        dve.wait_ge(s["sb_ln"], it * 2 + (h + 1))
                        v.scalar_tensor_tensor(sb_sp[:, h, :], ps[:, 4 + h, 0:3 * P], 0.0, sb_l[:, h, :],
                                               ALU.max, ALU.add).then_inc(s["sb_sp0"], 1)
                    for h in range(2):
                        dve.wait_ge(s["sb_sp0"], it * 2 + (h + 1))
                        v.tensor_tensor(sb_sp[:, h, :], sb_sp[:, h, :], const("sb_mask"), ALU.mult).then_inc(s["sb_sp1"], 1)

                def weights():
                    for h in range(2):
                        dve.wait_ge(s["sb_aexp"], it * 2 + (h + 1))
                        v.scalar_tensor_tensor(sb_a[:, h, :], sb_a[:, h, :], BIG, const("sb_mask"),
                                               ALU.min, ALU.mult).then_inc(s["sb_am"], 1)

                def values():
                    take(c + 2, 0, tmp[:, 0])
                    v.tensor_tensor(sb_v, tmp[:, 0], rs_col2, ALU.mult).then_inc(s["sb_vr"], 1)

                def gate():
                    t = tmp[:, 1]
                    take(c + 3, 1, t)
                    v.tensor_tensor(t, t, rs_row2, ALU.mult).then_inc(s["sb_gate"], 1)

                def outputs():
                    t = tmp[:, 1]
                    dve.wait_ge(s["sb_gsig"], it + 1)
                    v.tensor_tensor(t, t, sb_sg, ALU.mult).then_inc(s["sb_gg"], 1)
                    dve.wait_ge(s["sb_gg"], it + 1)
                    dve.wait_ge(s["sb_av"], it + 1)
                    v.tensor_tensor(t, ps[:, 6, :].rearrange("p (a b) -> p a b", a=2), t, ALU.mult).then_inc(s["sb_y"], 1)
                    dve.wait_ge(s["y_hi"], it + 9)
                    v.tensor_tensor(ypair[:, bass.ds(it * 2, 2), 1, :], t,
                                    ypair[:, bass.ds(it * 2, 2), 0, :].bitcast(F32), ALU.subtract).then_inc(ypair_ready, 1)

                slot(c, ((END, queries),))
                slot(c + 1, ((END, keys),))
                slot(c + 2, ((1, softplus), (END, values)))
                slot(c + 3, ((0, weights), (END, gate), (3, outputs)))

            out_stage(C_OUT1)
            xq_stage(C_XQ1, XA_HEADS, 5)
            def last_residual():
                dve.wait_ge(s["xg_ready"], 24 + 7)
                v.tensor_tensor(xT[:, KT - 2:KT, :], xT[:, KT - 2:KT, :], tmp[:, 1], ALU.add).then_inc(s["x_new"], 1)
                dve.wait_ge(s["x_new"], 24 + 8)
                for k in range(KT - 2, KT):
                    last = v.tensor_scalar(xkT[:, k, :], xT[:, k, :], prm("final", k, 1), None, ALU.mult)
                last.then_inc(s["xg_ready"], 1)

            out_stage(C_OX1, heads=XA_HEADS, pair=False, after=last_residual)
            dve.wait_ge(s["stats_done"], 6)
            v.tensor_scalar(rs_col, ps[:, 7, S:S + 2], 1.0 / D, EPS, ALU.mult, ALU.add).then_inc(s["rs_raw"], 1)
            dve.wait_ge(s["rs_root"], 6)
            v.reciprocal(rs_col, rs_col).then_inc(s["rs_ready"], 1)
            dve.wait_ge(s["rs_ready"], 6)
            for half in range(2):
                for r in range(2):
                    q = 2 * half + 1
                    dve.wait_ge(s["fin_tr"], FINAL_ORDER[r, q] + 1)
                    v.tensor_scalar(xv[:, r, q * 512:(q + 1) * 512], ps[:, FINAL_BANK[r, q], :],
                                    rs_col[:, r:r + 1], None, ALU.mult).then_inc(fin_out[half][r], 1)

        @block.gpsimd
        def _(pool):
            g = nc.gpsimd
            sq_count = [0]

            def zero_acc(n):
                if n:
                    pool.wait_ge(s["stats_done"], n + 2)
                g.memset(acc[:], 0.0).then_inc(s["acc_zero"], 1)
                pool.wait_ge(s["acc_zero"], n + 1)

            def add_squares(block_ap, it, n0, last=False):
                g.tensor_tensor(sq[:], block_ap, block_ap, ALU.mult).then_inc(s["x_sq"], 1)
                pool.wait_ge(s["x_sq"], it + (n0 + 1))
                ins = g.tensor_tensor(acc[:], acc[:], sq[:], ALU.add)
                return ins

            def out_stage(c0, gain, n_stats, n0, final=False, heads=None):
                zero_acc(n_stats)

                def residual(it, j):
                    i = it * 2 + j
                    blk = bass.ds(it * 4 + 2 * j, 2)
                    pool.wait_ge(s["out_tmp"], i + (n0 + 1))
                    g.tensor_tensor(xT[:, blk, :], xT[:, blk, :], tmp[:, j], ALU.add).then_inc(s["x_new"], 1)
                    pool.wait_ge(s["x_new"], i + (n0 + 1))
                    o, _ = PARAMS[gain]
                    gb = par[:, bass.ds(it * 4 + (2 * j + o), 2)].unsqueeze(2).to_broadcast([P, 2, S])
                    dst = xkT[:, blk, :] if final else out_xg
                    g.tensor_tensor(dst, xT[:, blk, :], gb, ALU.mult).then_inc(s["xg_ready"], 1)
                    add_squares(xT[:, blk, :], i, n0).then_inc(s["xt_done"], 1)
                    pool.wait_ge(s["xt_done"], i + (n0 + 1))

                if heads is not None:
                    residual(0, 0)
                    residual(0, 1)
                with pool.Fori(0 if heads is None else 1, 3 if final else 4, 1) as it:
                    for j in range(2):
                        residual(it, j)
                if final:
                    residual(3, 0)
                pool.nop().then_inc(s["acc_ready"], 1)

            def copy_values(base, h):
                n = h + (base + 1)
                g.tensor_copy(xq_v, xv[:, :, bass.ds(h * 512, 512)]).then_inc(s["xa_vcopy"], 1)

            def xq_stage(base):
                copy_values(base, 0)
                with pool.Fori(1, XA_HEADS, 1) as it:
                    pool.wait_ge(s["xa_pv"], (it + base) * 2)
                    copy_values(base, it)

            pool.wait_ge(s["squares_done"], 4)
            pool.wait_ge(s["tr_done"], 16)
            g.memset(pool_cs[:, :, 0:PAD], 0.0).then_inc(s["cs_zero"], 1)
            pool.wait_ge(pool_in, 32)
            for n in range(4):
                pool.wait_ge(s["cs_ready"], n + 1)
                cs = pool_cs[:, 2 * n:2 * n + 2, :]
                w = WINDOWS[n]
                u = pool_u[:, 2 * n:2 * n + 2, :]
                g.tensor_tensor(sq[:], cs[:, :, PAD:], cs[:, :, PAD - w:PAD - w + S], ALU.subtract).then_inc(s["diff_ready"], 1)
                pool.wait_ge(s["diff_ready"], n + 1)
                g.tensor_tensor(sq[:], sq[:], pool_inv[:, n, :].unsqueeze(1).to_broadcast([P, 2, S]), ALU.mult).then_inc(s["diff_scaled"], 1)
                pool.wait_ge(s["diff_scaled"], n + 1)
                g.tensor_tensor(u, sq[:], u, ALU.subtract).then_inc(s["mixed_ready"], 1)
                pool.wait_ge(s["mixed_ready"], n + 1)

            with pool.Fori(0, 4, 1) as it:
                pool.wait_ge(s["hg_values"], it + 1)
                pool.wait_ge(s["hg_keys"], it + 1)
                for t in range(2):
                    last = g.tensor_tensor(hg_bd[:, t], hg_i[:, t, :].unsqueeze(1).to_broadcast([P, 4, CH]),
                                           const("chunk_mask").unsqueeze(2).to_broadcast([P, 4, CH]), ALU.mult)
                last.then_inc(s["hg_bd_ready"], 1)
                pool.wait_ge(s["hg_gsig"], it + 1)
                g.tensor_tensor(tmp[:, 1], tmp[:, 1], hg_sg, ALU.mult).then_inc(s["hg_gg0"], 1)
                pool.wait_ge(s["hg_gg0"], it + 1)
                o, _ = PARAMS["hgrn_g"]
                g.tensor_tensor(tmp[:, 1], tmp[:, 1], par[:, bass.ds(it * 2 + o, 2)].unsqueeze(2).to_broadcast([P, 2, S]),
                                ALU.mult).then_inc(s["hg_gg1"], 1)

            out_stage(C_OUT0, "xa0", 0, 0)
            xq_stage(0)
            out_stage(C_OX0, "mix1", 1, 8, heads=0)
            out_stage(C_OUT1, "xa1", 2, 16)
            xq_stage(XA_HEADS)
            out_stage(C_OX1, "final", 3, 24, final=True, heads=XA_HEADS)


def constants():
    import numpy as np
    p = np.arange(P)[:, None]
    j = np.arange(P)[None, :]
    t = np.arange(S)[None, :]
    parts = {
        "ident": p == j,
        "ones": np.ones((P, P)),
        "neg_tri": -1.0 * (p >= j),
        "neg_ones": -np.ones((P, P)),
        "sb_mask": np.concatenate([p < j, np.ones((P, P)), p < j], 1),
        "hg_mask": (p <= j) & (p // HC == j // HC),
        "reset": np.broadcast_to(t % HC != 0, (P, S)),
        "chunk_mask": p // HC == np.arange(P // HC)[None, :],
    }
    inv = np.stack([1.0 / np.minimum(np.arange(1, S + 1), w) for w in WINDOWS])
    return (np.concatenate([np.asarray(parts[n], np.float32) for n in CONSTS], 1),
            np.ascontiguousarray(np.broadcast_to(inv.astype(np.float32), (P, 4, S))))


def kernel(**inputs):
    import numpy as np
    import concourse.bacc as bacc
    from concourse.bass_utils import run_bass_kernel_spmd

    a = {n: np.ascontiguousarray(v) for n, v in inputs.items()}
    tables, inv_count = constants()

    def columns(v):
        return v.reshape(-1, P).T

    rows = {
        "mix0": a["norm_mix_g"][0], "mix1": a["norm_mix_g"][1], "xa0": a["norm_xa_g"][0], "xa1": a["norm_xa_g"][1],
        "mem0": a["norm_mem_g"][0], "mem1": a["norm_mem_g"][1], "final": a["final_norm_g"],
        "pool_scale": a["pool_scale"][0], "bound0": a["hgrn_lower_bounds"][0], "bound1": a["hgrn_lower_bounds"][1],
        "hgrn_g": a["hgrn_norm_g"][0],
    }
    arrays = {
        "x": a["x"], "mem": a["mem"],
        "params": np.ascontiguousarray(np.concatenate([columns(rows[n]) for n in PARAMS], 1)),
        "consts": tables, "inv_count": inv_count, "pool_w": a["pool_w"],
        "w_in_even": a["w_in_even"], "w_out_even": a["w_out_even"], "w_in_odd": a["w_in_odd"],
        "w_out_odd": a["w_out_odd"], "xa_wq": a["xa_wq"], "xa_wkv": a["xa_wkv"], "xa_wo": a["xa_wo"],
    }
    nc = bacc.Bacc("TRN2", target_bir_lowering=False, num_devices=1)
    handles = [nc.dram_tensor(n, v.shape, F32, kind="ExternalInput").ap() for n, v in arrays.items()]
    out = nc.dram_tensor("out", (1, S, D), F32, kind="ExternalOutput").ap()
    build(nc, *handles, out)
    result = run_bass_kernel_spmd(nc, [arrays], core_ids=[0])
    return result.results[0]["out"]
```
